# Optimizing a Trainium2 kernel written in Bass

```python
import jax, jax.numpy as jnp
from jax import lax
import numpy as np

D_MODEL = 1024
BATCH = 1
SEQ = 1024
DEPTH = 2

GRID_W = 64
CTX_LEN = 256
N_MIXERS = 3
EPS = 1e-6
N_MOD = 6
N_HEADS = 16
HEAD_DIM = D_MODEL // N_HEADS
N_KV_HEADS = 4
Q_GROUP = N_HEADS // N_KV_HEADS
Q_BLOCK = 128
ROPE_THETA = 10000.0
POOL_WINDOWS = (2, 4, 8, 16)
N_POOL_GROUPS = len(POOL_WINDOWS)
POOL_GROUP_DIM = D_MODEL // N_POOL_GROUPS
SGU_CHUNK = 128
SGU_WIDTH = D_MODEL
SGU_GROUPS = 8
SGU_GROUP_DIM = SGU_WIDTH // SGU_GROUPS
FFN_HIDDEN = 2816
CONV_WIDTH = 3

kernel_name = "hybrid_interleaved_diffusion_trunk"

def rmsnorm(x, g):
    xf = x.astype(jnp.float32)
    y = xf * lax.rsqrt(jnp.mean(xf * xf, axis=-1, keepdims=True) + EPS)
    return (y * g.astype(jnp.float32)).astype(x.dtype)

def modulation(vec, w, b):
    mod = (jax.nn.silu(vec) @ w + b)[:, None, :]
    return jnp.split(mod, N_MOD, axis=-1)

def modulate(h, shift, scale):
    return h * (1 + scale) + shift

def axial_tables(length, dtype):
    rows = length // GRID_W
    row = jnp.repeat(jnp.arange(rows), GRID_W).astype(jnp.float32)
    col = jnp.tile(jnp.arange(GRID_W), rows).astype(jnp.float32)
    n_freq = HEAD_DIM // 4
    freqs = ROPE_THETA ** (-jnp.arange(n_freq, dtype=jnp.float32) / n_freq)
    ang_r = row[:, None] * freqs
    ang_c = col[:, None] * freqs
    tab = lambda a: (jnp.cos(a)[None, :, None, :].astype(dtype), jnp.sin(a)[None, :, None, :].astype(dtype))
    return tab(ang_r), tab(ang_c)

def _rotate(u, cos, sin):
    n = u.shape[-1] // 2
    u1, u2 = u[..., :n], u[..., n:]
    return jnp.concatenate([u1 * cos - u2 * sin, u2 * cos + u1 * sin], axis=-1)

def rope_2d(x, tables):
    (cr, sr), (cc, sc) = tables
    half = HEAD_DIM // 2
    return jnp.concatenate([_rotate(x[..., :half], cr, sr), _rotate(x[..., half:], cc, sc)], axis=-1)

def attend(q, k, v):
    s = jnp.einsum('bqkgd,bskd->bkgqs', q, k).astype(jnp.float32) * (HEAD_DIM ** -0.5)
    p = jax.nn.softmax(s, axis=-1).astype(v.dtype)
    return jnp.einsum('bkgqs,bskd->bqkgd', p, v)

def attention_mixer(hx, hc, wqkv, q_gain, k_gain, wo, need_ctx):
    B, L, _ = hx.shape
    Lc = hc.shape[1]
    nq, nk = N_HEADS * HEAD_DIM, N_KV_HEADS * HEAD_DIM

    def project(h):
        qkv = h @ wqkv
        n = h.shape[1]
        q = qkv[..., :nq].reshape(B, n, N_HEADS, HEAD_DIM)
        k = qkv[..., nq:nq + nk].reshape(B, n, N_KV_HEADS, HEAD_DIM)
        v = qkv[..., nq + nk:].reshape(B, n, N_KV_HEADS, HEAD_DIM)
        return rmsnorm(q, q_gain), rmsnorm(k, k_gain), v

    qx, kx, vx = project(hx)
    qc, kc, vc = project(hc)
    tables = axial_tables(L, hx.dtype)
    qx, kx = rope_2d(qx, tables), rope_2d(kx, tables)

    k_all = jnp.concatenate([kc, kx], axis=1)
    v_all = jnp.concatenate([vc, vx], axis=1)
    nb = L // Q_BLOCK
    qb = qx.reshape(B, nb, Q_BLOCK, N_KV_HEADS, Q_GROUP, HEAD_DIM).transpose(1, 0, 2, 3, 4, 5)
    ob = lax.map(lambda q: attend(q, k_all, v_all), qb)
    ox = ob.transpose(1, 0, 2, 3, 4, 5).reshape(B, L, nq) @ wo
    if not need_ctx:
        return ox, None
    oc = attend(qc.reshape(B, Lc, N_KV_HEADS, Q_GROUP, HEAD_DIM), kc, vc).reshape(B, Lc, nq) @ wo
    return ox, oc

def pool_mixer(h, w, b, scale):
    B, L, C = h.shape
    cs = jnp.cumsum(h.astype(jnp.float32), axis=1)
    cs = jnp.concatenate([jnp.zeros((B, 1, C), jnp.float32), cs], axis=1)
    t = jnp.arange(L)
    outs = []
    for g, win in enumerate(POOL_WINDOWS):
        lo = jnp.maximum(t - win // 2, 0)
        hi = jnp.minimum(t + win - win // 2 - 1, L - 1)
        sl = cs[..., g * POOL_GROUP_DIM:(g + 1) * POOL_GROUP_DIM]
        s = jnp.take(sl, hi + 1, axis=1) - jnp.take(sl, lo, axis=1)
        cnt = (hi - lo + 1).astype(jnp.float32)[None, :, None]
        outs.append(s / cnt)
    pooled = jnp.concatenate(outs, axis=-1).astype(h.dtype) - h
    y = jnp.einsum('blgd,gde->blge', pooled.reshape(B, L, N_POOL_GROUPS, POOL_GROUP_DIM), w).reshape(B, L, C) + b
    return y * scale

def sgu_mixer(h, w_in, v_gain, w_s, b_s, w_out):
    B, L, _ = h.shape
    z = jax.nn.gelu(h @ w_in)
    u, v = z[..., :SGU_WIDTH], z[..., SGU_WIDTH:]
    v = rmsnorm(v, v_gain)
    nc = L // SGU_CHUNK
    vv = v.reshape(B, nc, SGU_CHUNK, SGU_GROUPS, SGU_GROUP_DIM)
    y = jnp.einsum('gmn,bcnge->bcmge', w_s, vv) + b_s.T[None, None, :, :, None]
    return (u * y.reshape(B, L, SGU_WIDTH)) @ w_out

def dwconv(a, w, b):
    L = a.shape[1]
    p = CONV_WIDTH // 2
    ap = jnp.pad(a, ((0, 0), (p, CONV_WIDTH - 1 - p), (0, 0)))
    return sum(ap[:, k:k + L] * w[k] for k in range(CONV_WIDTH)) + b

def conv_ffn(h, w_up, conv_w, conv_b, w_down):
    a = dwconv(h @ w_up, conv_w, conv_b)
    val, gate = a[..., :FFN_HIDDEN], a[..., FFN_HIDDEN:]
    return (jax.nn.silu(gate) * val) @ w_down

def setup_inputs(seed: int = 0) -> dict:
    key = jax.random.key(seed)
    ks = iter(jax.random.split(key, 32))
    D, F = D_MODEL, FFN_HIDDEN
    n_a = len(range(0, DEPTH, N_MIXERS))
    n_b = len(range(1, DEPTH, N_MIXERS))
    n_c = len(range(2, DEPTH, N_MIXERS))
    nrm = lambda shape, s: jax.random.normal(next(ks), shape, jnp.float32) * s
    gain = lambda shape: 1.0 + nrm(shape, 0.02)
    qkv_w = (N_HEADS + 2 * N_KV_HEADS) * HEAD_DIM
    return {
        "x": nrm((BATCH, SEQ, D), 1.0),
        "c": nrm((BATCH, D), 1.0),
        "ctx": nrm((BATCH, CTX_LEN, D), 1.0),
        "c_ctx": nrm((D,), 1.0),
        "ada_w": nrm((DEPTH, D, N_MOD * D), 0.5 * D ** -0.5),
        "ada_b": nrm((DEPTH, N_MOD * D), 0.02),
        "norm_w": gain((DEPTH, 2, D)),
        "attn_wqkv": nrm((n_a, D, qkv_w), D ** -0.5),
        "attn_q_gain": gain((n_a, HEAD_DIM)),
        "attn_k_gain": gain((n_a, HEAD_DIM)),
        "attn_wo": nrm((n_a, N_HEADS * HEAD_DIM, D), (N_HEADS * HEAD_DIM) ** -0.5),
        "pool_w": nrm((n_b, N_POOL_GROUPS, POOL_GROUP_DIM, POOL_GROUP_DIM), POOL_GROUP_DIM ** -0.5),
        "pool_b": nrm((n_b, D), 0.02),
        "pool_scale": 1.0 + nrm((n_b, D), 0.1),
        "sgu_w_in": nrm((n_c, D, 2 * SGU_WIDTH), D ** -0.5),
        "sgu_v_gain": gain((n_c, SGU_WIDTH)),
        "sgu_w_s": nrm((n_c, SGU_GROUPS, SGU_CHUNK, SGU_CHUNK), SGU_CHUNK ** -0.5),
        "sgu_b_s": 1.0 + nrm((n_c, SGU_GROUPS, SGU_CHUNK), 0.1),
        "sgu_w_out": nrm((n_c, SGU_WIDTH, D), SGU_WIDTH ** -0.5),
        "ffn_w_up": nrm((DEPTH, D, 2 * F), D ** -0.5),
        "ffn_conv_w": nrm((DEPTH, CONV_WIDTH, 2 * F), CONV_WIDTH ** -0.5),
        "ffn_conv_b": nrm((DEPTH, 2 * F), 0.02),
        "ffn_w_down": nrm((DEPTH, F, D), F ** -0.5),
        "final_norm": gain((D,)),
    }

def reference(x, c, ctx, c_ctx, ada_w, ada_b, norm_w, attn_wqkv, attn_q_gain, attn_k_gain, attn_wo,
              pool_w, pool_b, pool_scale, sgu_w_in, sgu_v_gain, sgu_w_s, sgu_b_s, sgu_w_out,
              ffn_w_up, ffn_conv_w, ffn_conv_b, ffn_w_down, final_norm):
    xc = ctx
    c_vec = c_ctx[None, :]
    for i in range(DEPTH):
        kind, j, last = i % N_MIXERS, i // N_MIXERS, i == DEPTH - 1
        sh1, sc1, g1, sh2, sc2, g2 = modulation(c, ada_w[i], ada_b[i])
        csh1, csc1, cg1, csh2, csc2, cg2 = modulation(c_vec, ada_w[i], ada_b[i])
        hx = modulate(rmsnorm(x, norm_w[i, 0]), sh1, sc1)
        hc = modulate(rmsnorm(xc, norm_w[i, 0]), csh1, csc1)
        if kind == 0:
            dx, dc = attention_mixer(hx, hc, attn_wqkv[j], attn_q_gain[j], attn_k_gain[j], attn_wo[j],
                                     need_ctx=not last)
        elif kind == 1:
            dx = pool_mixer(hx, pool_w[j], pool_b[j], pool_scale[j])
            dc = None if last else pool_mixer(hc, pool_w[j], pool_b[j], pool_scale[j])
        else:
            dx = sgu_mixer(hx, sgu_w_in[j], sgu_v_gain[j], sgu_w_s[j], sgu_b_s[j], sgu_w_out[j])
            dc = None if last else sgu_mixer(hc, sgu_w_in[j], sgu_v_gain[j], sgu_w_s[j], sgu_b_s[j], sgu_w_out[j])
        x = x + g1 * dx
        hx2 = modulate(rmsnorm(x, norm_w[i, 1]), sh2, sc2)
        x = x + g2 * conv_ffn(hx2, ffn_w_up[i], ffn_conv_w[i], ffn_conv_b[i], ffn_w_down[i])
        if not last:
            xc = xc + cg1 * dc
            hc2 = modulate(rmsnorm(xc, norm_w[i, 1]), csh2, csc2)
            xc = xc + cg2 * conv_ffn(hc2, ffn_w_up[i], ffn_conv_w[i], ffn_conv_b[i], ffn_w_down[i])
    return rmsnorm(x, final_norm)


_drawn_inputs = setup_inputs


def setup_inputs(seed=0):
    import zlib

    import numpy as np

    out = dict(_drawn_inputs(seed))
    spreads = {}
    factors = {'ctx': 8.0,
     'c_ctx': 2.861,
     'norm_w': 5.513,
     'attn_q_gain': 8.0,
     'attn_k_gain': 8.0,
     'pool_b': 64.0,
     'ffn_conv_b': 6.916,
     'final_norm': 8.16}
    for name, (base, spread) in spreads.items():
        noise = np.random.default_rng([zlib.crc32(name.encode()), seed]).standard_normal(out[name].shape)
        drawn = base * np.exp(spread * noise) if base else spread * noise
        out[name] = __import__('jax').numpy.asarray(drawn.astype(out[name].dtype))
    for name, factor in factors.items():
        out[name] = (out[name] * factor).astype(out[name].dtype)
    return out
```

```python
import concourse.bass as bass
from concourse import mybir
from contextlib import ExitStack


def hybrid_trunk(nc, x, c, ctx, c_ctx, ada_w, ada_b, norm_w, wqkv, q_gain, k_gain, wo,
                 pool_w, pool_b, pool_scale, w_up, conv_w, conv_b, w_down, final_norm,
                 rope_cos, rope_sin, pool_edge, out):
    fp32 = mybir.dt.float32
    fp32r = mybir.dt.float32r
    ALU = mybir.AluOpType
    ACT = mybir.ActivationFunctionType
    AX = mybir.AxisListType

    P = 128
    NT, D = x.shape[1], x.shape[2]
    NC = ctx.shape[1]
    TT, CT, FT = NT // P, NC // P, D // P
    KT = TT + CT
    NK = KT * P
    HD = q_gain.shape[1]
    NH = wo.shape[1] // HD
    NKV = (wqkv.shape[2] // HD - NH) // 2
    GQ = NH // NKV
    HALF = 512
    FH = w_down.shape[1]
    HT = FH // P
    NI = HT // 2
    UC = 256
    MT = 6 * FT
    NU = 6 * D // UC
    EPS = 1e-6
    SCALE = float(HD) ** -0.5
    WINDOWS = (2, 4, 8, 16)
    PAD = WINDOWS[-1] // 2
    VW = 2 * HD + 2

    U_K, U_V, U_Q, U_WO = 0, 1, 2, 6
    NQU = NH * HD // UC
    NWO = D // UC
    U_F0 = U_WO + NWO
    U_POOL = U_F0 + 3 * NI
    U_F1 = U_POOL + 1

    KB = 1024
    base = (nc.sbuf_base + 63) // 64 * 64
    es = ExitStack()
    with es:
        def at(name, shape, off, dt=fp32):
            return nc.alloc_sbuf_tensor_at(name, shape, dt, offset=base + int(off))

        def sem(name):
            return es.enter_context(nc.semaphore(name))

        h_hi = at("h_hi", [P, FT, NT], 0, fp32r)
        h_lo = at("h_lo", [P, FT, NT], 32 * KB, fp32r)
        junk = at("junk", [P, D], 0)
        qa = [at(f"qa{i}", [P, NT], 4 * KB * i, fp32r) for i in range(2)]
        qb = [at(f"qb{i}", [P, NT], (8 + 4 * i) * KB, fp32r) for i in range(2)]
        ka = [at(f"ka{i}", [P, NK], (16 + 5 * i) * KB, fp32r) for i in range(2)]
        kb = [at(f"kb{i}", [P, NK], (26 + 5 * i) * KB, fp32r) for i in range(2)]
        p_hi = [at(f"p_hi{i}", [P, 2 * HALF], (36 + 4 * i) * KB, fp32r) for i in range(3)]
        p_lo = [at(f"p_lo{i}", [P, 2 * HALF], (48 + 4 * i) * KB, fp32r) for i in range(3)]
        o_t = [at(f"o_t{i}", [P, HALF], (60 + 2 * i) * KB) for i in range(2)]
        raw = [at("raw0", [P, FT * UC], 64 * KB), at("raw1", [P, FT * UC], 72 * KB),
               at("raw2", [P, FT * UC], 80 * KB)]
        ada_raw = [at("ada_raw0", [P, FT, UC], 80 * KB), at("ada_raw1", [P, FT, UC], 88 * KB)]
        y_val = [at(f"y_val{j}", [P, NT], (88 + 4 * j) * KB) for j in range(2)]
        w_hi = [at(f"w_hi{i}", [P, FT * UC], (96 + 16 * i) * KB, fp32r) for i in range(3)]
        w_lo = [at(f"w_lo{i}", [P, FT * UC], (104 + 16 * i) * KB, fp32r) for i in range(3)]
        x_tok = at("x_tok", [P, TT, D], 128 * KB)
        q_tok = at("q_tok", [P, TT, D], 128 * KB)
        ch_hi = at("ch_hi", [P, FT, NC], 128 * KB, fp32r)
        ch_lo = at("ch_lo", [P, FT, NC], 136 * KB, fp32r)
        xT = at("xT", [P, FT, NT], 144 * KB)
        k_tok = at("k_tok", [P, KT, NKV * HD], 160 * KB)
        c_tok = at("c_tok", [P, CT, D], 160 * KB)
        v_hl = at("v_hl", [P, KT, NKV, VW], 170 * KB, fp32r)
        rows = at("rows", [P, 4, P], 170 * KB)
        cosT = at("cosT", [P, TT, HD], 172 * KB)
        sinT = at("sinT", [P, TT, HD], 174 * KB)
        gains = at("gains", [P, 2, HD], 176 * KB)
        x_re = at("x_re", [P, TT // 2, D], 176 * KB)
        t_buf = [at(f"t_buf{i}", [P, NT], (176 + 4 * i) * KB) for i in range(2)]
        y_gate = [at(f"y_gate{j}", [P, NT], (176 + 4 * j) * KB) for j in range(2)]
        sq = [at(f"sq{i}", [P, NT], (184 + 4 * i) * KB) for i in range(4)]
        g_hi = at("g_hi", [P, 2, NT], 184 * KB, fp32r)
        g_lo = at("g_lo", [P, 2, NT], 192 * KB, fp32r)
        PW = NT + 2 * PAD
        hp = at("hp", [P, PW], 184 * KB)
        win = [at(f"win{i}", [P, PW], 184 * KB + (i + 1) * 4 * PW) for i in range(2)]
        o_sb = [at(f"o_sb{i}", [P, D], (4 * i) * KB) for i in range(2)]
        tabs = [at(f"tab{i}", [P, TT, HD], (191 + 2 * i) * KB) for i in range(4)]
        p32 = [at(f"p32_{i}", [P, 2 * HALF], (191 + 4 * i) * KB) for i in range(2)]
        acc = [at(f"acc{i}", [P, UC], (199 + i) * KB) for i in range(2)]
        id_r = at("id_r", [P, P], 199 * KB, fp32r)
        s1 = at("s1", [P, HALF], 201 * KB)
        s2 = at("s2", [P, HALF], 203 * KB)
        accc = [at(f"accc{i}", [P, UC], (201 + i) * KB) for i in range(2)]
        t0 = [s1, s2]
        off = [205 * KB]

        def small(name, cols, dt=fp32):
            t = at(name, [P, cols], off[0], dt)
            off[0] += (4 * cols + 31) // 32 * 32
            return t

        NCONV = 4 * 2 * HT
        cst = small("cst", 2 * MT + 7 * FT + NCONV)
        C_NW, C_PB, C_PS, C_FN, C_CV = 2 * MT, 2 * MT + 4 * FT, 2 * MT + 5 * FT, 2 * MT + 6 * FT, 2 * MT + 7 * FT
        CV_W = [C_CV, C_CV + 2 * HT, C_CV + 4 * HT]
        CV_B = C_CV + 6 * HT
        ident = small("ident", P)
        one = small("one", 1)
        eps = small("eps", 1)
        mod = [small("mod0", MT), small("mod1", MT)]
        modc = small("modc", 2 * FT)
        nA = [small(f"nA{i}", FT) for i in range(5)]
        gs = small("gs", FT)
        gb = small("gb", FT)
        cvec = small("cvec", 2 * FT)
        csil = small("csil", 2 * FT)
        ss = small("ss", KT)
        std = small("std", KT)
        rstd = small("rstd", KT)
        mx = [at(f"mx{i}", [P, 3 * TT], 199.5 * KB + 96 * i) for i in range(2)]
        mxr = at("mxr", [P, TT], 199.5 * KB + 192)
        mneg = [at(f"mneg{i}", [P, TT], 199.5 * KB + 224 + 32 * i, fp32r) for i in range(2)]
        rden = at("rden", [P, 4], 199.5 * KB + 288)
        edge = at("edge", [P, 4 * 2 * PAD], 201 * KB)
        assert base + off[0] <= nc.sbuf_usable_end, (base + off[0], nc.sbuf_usable_end)

        ps = es.enter_context(nc.psum_tensor("ps", [P, 8, HALF], fp32))

        def wide(b, n=2):
            return ps[:, b:b + n, :].rearrange("p a b -> p (a b)")

        rows_in = sem("rows_in"); c_in = sem("c_in"); gain_in = sem("gain_in"); rope_in = sem("rope_in")
        x_in = [sem("x_in0"), sem("x_in1")]; ctx_in = sem("ctx_in"); conv1_in = sem("conv1_in")
        edge_in = sem("edge_in"); xre_in = sem("xre_in"); out_done = [sem("out_done0"), sem("out_done1")]
        ada_in = [sem("ada_in0"), sem("ada_in1")]
        raw_in = [sem(f"raw_in{i}") for i in range(3)]
        hi_step = sem("hi_step")
        unit_here = sem("unit_here")
        w_split = sem("w_split")
        id_ready = sem("id_ready"); cst_init = sem("cst_init"); rows_t = sem("rows_t"); cst_ready = sem("cst_ready")
        csil_ready = sem("csil_ready"); vstep = sem("vstep"); astep = sem("astep")
        ada_acc = sem("ada_acc"); ada_sum = sem("ada_sum"); mod_ready = sem("mod_ready")
        x_sq = sem("x_sq"); x_rstd = sem("x_rstd"); x_scaled = sem("x_scaled")
        xt_ready = sem("xt_ready"); t_ready = sem("t_ready"); h_split = sem("h_split")
        blk = sem("blk"); kq_out = sem("kq_out"); ssq_ready = sem("ssq_ready"); kq_std = sem("kq_std")
        roped = sem("roped"); v_hi_ready = sem("v_hi_ready"); v_out = sem("v_out"); tab_ready = sem("tab_ready")
        kT_ready = sem("kT_ready"); k_hi_ready = sem("k_hi_ready"); k_lo_ready = sem("k_lo_ready")
        qT_ready = sem("qT_ready"); q_hi_ready = sem("q_hi_ready"); q_lo_ready = sem("q_lo_ready")
        mx_ps = sem("mx_ps"); mx_red = sem("mx_red"); mneg_ready = sem("mneg_ready")
        mrow_ps = sem("mrow_ps"); mrow_ready = sem("mrow_ready")
        s_ps = sem("s_ps"); p_ready = sem("p_ready"); phi_ready = sem("phi_ready"); plo_ready = sem("plo_ready"); plo2_ready = sem("plo2_ready")
        pv_step = sem("pv_step"); o_copied = sem("o_copied"); o_turned = sem("o_turned"); o_ready = sem("o_ready")
        oT_ps = sem("oT_ps"); oT_hi = sem("oT_hi"); oT_lo = sem("oT_lo")
        xr_ps = sem("xr_ps"); xr_out = sem("xr_out"); wo_ps = sem("wo_ps"); wo_out = sem("wo_out")
        sq_ready = sem("sq_ready"); sq_used = sem("sq_used"); ss_std = sem("ss_std"); ss_rstd = sem("ss_rstd")
        bc_ready = sem("bc_ready"); nt_ready = sem("nt_ready"); n_hi = sem("n_hi"); n_lo = sem("n_lo")
        up_ps = sem("up_ps"); y_ready = sem("y_ready"); cv_half = sem("cv_half"); cv_done = sem("cv_done")
        silu_ready = sem("silu_ready"); g_ready = sem("g_ready"); g_hi_ready = sem("g_hi_ready"); g_lo_ready = sem("g_lo_ready")
        dn_ps = sem("dn_ps"); dn_out = sem("dn_out")
        hp_ready = sem("hp_ready"); pooled = sem("pooled"); pl_ps = sem("pl_ps"); pl_t = sem("pl_t"); pl_out = sem("pl_out")
        fin_scaled = sem("fin_scaled"); fin_ps = sem("fin_ps"); fin_out = sem("fin_out")

        NP_ = TT // 2
        BLKS = [(U_K, p) for p in range(NP_ + 1)] + [(U_V, p) for p in range(NP_ + 1)] \
            + [(U_Q + u, p) for u in range(NQU) for p in range(NP_)]
        KQ = [b for b, (u, _) in enumerate(BLKS) if u != U_V]
        VB = [b for b, (u, _) in enumerate(BLKS) if u == U_V]
        EARLY = 2 * D // UC
        ADA_AT = {b: EARLY + b - 1 for b in range(1, NU - EARLY + 1)}
        NG = NWO * 4
        WO_ADA, n = [], NU
        for g in range(NG):
            k = 2 - g % 2
            WO_ADA.append(list(range(n, n + k)))
            n += k
        assert n == 2 * NU
        SLOT = [u % 2 for u in range(U_F0)] + ([0, 1] + [0, 2, 1] * (NI - 1) + [2]) + [0] + ([0, 1] + [0, 2, 1] * (NI - 1) + [2])
        NUNITS = len(SLOT)

        def nth(u):
            same = [v for v in range(u + 1) if SLOT[v] == SLOT[u]]
            return len(same), (same[-2] if len(same) > 1 else None)

        def cols_of(w, c0):
            return w[:, c0:c0 + UC].rearrange("(t p) n -> p t n", p=P)

        def unit_src(u):
            if u == U_K:
                return cols_of(wqkv[0], NH * HD)
            if u == U_V:
                return cols_of(wqkv[0], (NH + NKV) * HD)
            if u < U_WO:
                return cols_of(wqkv[0], (u - U_Q) * UC)
            if u < U_F0:
                return cols_of(wo[0], (u - U_WO) * UC)
            if u == U_POOL:
                return pool_w[0].rearrange("g (t p) e -> p (g t) e", p=P)

        def used(u):
            if u < U_WO:
                return blk, max(b for b, (v, _) in enumerate(BLKS) if v == u) + 1
            if u < U_F0:
                return wo_ps, 4 * (u - U_WO + 1)
            if u == U_POOL:
                return pl_ps, 2 * FT
            l, v = (0, u - U_F0) if u < U_POOL else (1, u - U_F1)
            if v == 3 * NI - 1:
                return dn_ps, 2 * FT * NI * (l + 1)
            i, kind = (0, 2 * v) if v < 2 else ((v + 1) // 3, (v + 1) % 3)
            assert kind != 1
            return up_ps, 4 * NI * l + 4 * i + kind + 2

        def raw3(s):
            return raw[s][:, :].rearrange("p (t n) -> p t n", n=UC)

        def hl(s):
            return (w_hi[s][:, :].rearrange("p (t n) -> p t n", n=UC),
                    w_lo[s][:, :].rearrange("p (t n) -> p t n", n=UC))

        def hl_down(s):
            return (w_hi[s][:, :].rearrange("p (t n) -> p t n", n=D),
                    w_lo[s][:, :].rearrange("p (t n) -> p t n", n=D))

        def heads(t):
            return t.rearrange("p a (h d) -> p a h d", d=HD)

        NS = KT
        HS = NS // 2
        NM = 3 * TT
        ROW = TURN_K = NS - 3
        TURN_Q = NS - 2
        LC = 640

        def pieces(s):
            h, e = divmod(s, NS)
            g, k = (h + 1, e + 1) if e < ROW else (h + 2, 0)
            return g, ([3 * k + i for i in range(3)] if g < NH and (e < ROW or e == NS - 1) else [])

        def new_k(s):
            h, e = divmod(s, NS)
            return (h + 2) // GQ if e == TURN_K and h + 2 < NH and (h + 2) % GQ == 0 else None

        FB = [U_F0, U_F1]

        block = es.enter_context(nc.Block())

        @block.sync
        def _(sp):
            def ada(u):
                l, v = divmod(u, NU)
                if u >= 2:
                    sp.wait_ge(ada_acc, u - 1)
                sp.dma_start(ada_raw[u % 2][:, :, :],
                             ada_w[l][:, v * UC:(v + 1) * UC].rearrange("(p t) n -> p t n", t=FT)
                             ).then_inc(ada_in[u % 2], 16)

            def load(u):
                n_, prev = nth(u)
                if prev is not None:
                    sp.wait_ge(w_split, prev + 1)
                sp.dma_start(raw3(SLOT[u]), unit_src(u)).then_inc(raw_in[SLOT[u]], 16)

            ada(0); ada(1)
            load(0)
            for u in range(2, EARLY):
                ada(u)
            load(1); load(2); load(3)
            for u in range(EARLY, NU):
                ada(u)
                if u == EARLY + 4:
                    load(4)
                if u == EARLY + 9:
                    load(5)
                if u == EARLY + 13:
                    load(6)
            load(7); load(8); load(9)
            ada(NU); ada(NU + 1)
            sp.wait_ge(pv_step, NH * NS)
            sp.dma_start(x_re[:, :, :], x[0, 0:NT // 2, :].rearrange("(t p) n -> p t n", p=P)).then_inc(xre_in, 16)
            sp.wait_ge(xr_ps, FT)
            sp.dma_start(x_re[:, :, :], x[0, NT // 2:NT, :].rearrange("(t p) n -> p t n", p=P)).then_inc(xre_in, 16)
            up0 = w_up[0]

            def load_up(l, s, col, n_wait):
                if n_wait is not None:
                    sp.wait_ge(w_split, n_wait)
                sp.dma_start(raw3(s), w_up[l][:, bass.ds(col, UC)].rearrange("(t p) n -> p t n", p=P)
                             ).then_inc(raw_in[s], 16)

            def load_down(l, row, n_wait):
                sp.wait_ge(w_split, n_wait)
                sp.dma_start(raw[2][:, :].rearrange("p (t n) -> p t n", n=D),
                             w_down[l][bass.ds(row, 2 * P), :].rearrange("(t p) n -> p t n", p=P)
                             ).then_inc(raw_in[2], 16)

            for u in range(NU + 2, 2 * NU):
                ada(u)
                if u == 2 * NU - 12:
                    load_up(0, 0, 0, nth(U_F0)[1] + 1)
                if u == 2 * NU - 6:
                    load_up(0, 1, FH, nth(U_F0 + 1)[1] + 1)
            sp.wait_ge(ada_acc, 2 * NU)
            for l in range(2):
                b = FB[l]
                if l == 1:
                    sp.wait_ge(w_split, nth(U_POOL)[1] + 1)
                    sp.dma_start(raw3(0), unit_src(U_POOL)).then_inc(raw_in[0], 16)
                    load_up(1, 0, 0, U_POOL + 1)
                    load_up(1, 1, FH, nth(U_F1 + 1)[1] + 1)
                with sp.Fori(1, NI) as i:
                    load_up(l, 0, i * UC, i * 3 + (b - 2))
                    load_down(l, (i - 1) * UC, i * 3 + (b - 2))
                    load_up(l, 1, i * UC + FH, i * 3 + (b - 1))
                load_down(l, (NI - 1) * UC, NI * 3 + b - 2)
            for t in range(TT):
                sp.wait_ge(fin_out, t + 1)
                sp.dma_start(out[0, t * P:(t + 1) * P, :], o_sb[t % 2][:, :]).then_inc(out_done[t % 2], 16)
            for o in out_done:
                sp.wait_ge(o, 16 * TT // 2)

        @block.gpsimd
        def _(pool):
            hs = [0]

            def split(dst_hi, dst_lo, src, done, k):
                pool.tensor_scalar(dst_hi, src, 1.0, 1.0, ALU.mult, ALU.mult).then_inc(hi_step, 1)
                pool.wait_ge(hi_step, k + 1)
                pool.tensor_tensor(dst_lo, src, dst_hi.bitcast(fp32), ALU.subtract).then_inc(done, 1)

            def split_unit(s, n_raw, last, k):
                pool.wait_ge(raw_in[s], n_raw)
                if last is not None:
                    pool.wait_ge(*last)
                pool.sem_inc(unit_here, 1)
                split(w_hi[s][:, :], w_lo[s][:, :], raw[s][:, :], w_split, k)

            pool.memset(ident[:, :], 0.0).then_inc(id_ready, 1)
            pool.wait_ge(id_ready, 1)
            pool.affine_select(out=ident[:, :], in_=ident[:, :], compare_op=ALU.not_equal, fill=1.0,
                               base=0, pattern=[[-1, P]], channel_multiplier=1).then_inc(id_ready, 1)
            for u in range(U_WO + 2):
                n_, prev = nth(u)
                split_unit(SLOT[u], 16 * n_, None if prev is None else used(prev), u)
            for s in range(NH * NS):
                pool.wait_ge(p_ready, s + 1)
                if s >= 3:
                    pool.wait_ge(pv_step, s - 2)
                pool.tensor_scalar(p_hi[s % 3][:, :], p32[s % 2][:, :], 1.0, 1.0, ALU.mult, ALU.mult
                                   ).then_inc(phi_ready, 1)
                pool.wait_ge(phi_ready, s + 1)
                pool.tensor_tensor(p_lo[s % 3][:, LC:], p32[s % 2][:, LC:], p_hi[s % 3][:, LC:].bitcast(fp32),
                                   ALU.subtract).then_inc(plo2_ready, 1)
            for u in range(U_WO + 2, U_F0 + 2):
                n_, prev = nth(u)
                split_unit(SLOT[u], 16 * n_, used(prev), u)
            for l in range(2):
                b = FB[l]
                if l == 1:
                    for u in (U_POOL, U_F1, U_F1 + 1):
                        n_, prev = nth(u)
                        split_unit(SLOT[u], 16 * n_, used(prev), u)
                nv, ng = nth(b)[0], nth(b + 1)[0]
                nd = nth(b + 3)[0]
                ub = 4 * NI * l
                with pool.Fori(1, NI) as i:
                    split_unit(0, i * 16 + 16 * nv, (up_ps, i * 4 + (ub - 2)), i * 3 + (b - 1))
                    split_unit(2, i * 16 + 16 * (nd - 1), (up_ps, i * 4 + (ub - 1)), i * 3 + b)
                    split_unit(1, i * 16 + 16 * ng, (up_ps, i * 4 + ub), i * 3 + (b + 1))
                split_unit(2, 16 * (nd - 1 + NI), (up_ps, NI * 4 + ub - 1), NI * 3 + b - 1)

        @block.scalar
        def _(act):
            for j, src in enumerate([ada_b.rearrange("l (j p) -> (l j) p", p=P)]):
                act.dma_start(rows[0:2 * MT, 0, :], src).then_inc(rows_in, 16)
            act.dma_start(rows[0:4 * FT, 1, :], norm_w.rearrange("l k (j p) -> (l k j) p", p=P)).then_inc(rows_in, 16)
            for n_, v in enumerate((pool_b[0], pool_scale[0], final_norm)):
                act.dma_start(rows[(4 + n_) * FT:(5 + n_) * FT, 1, :], v.rearrange("(j p) -> j p", p=P)).then_inc(rows_in, 16)
            cw0 = conv_w[0].rearrange("k (j p) -> (k j) p", p=P)
            cb0 = conv_b[0].rearrange("(j p) -> j p", p=P)
            act.dma_start(rows[0:4 * HT, 2, :], cw0[0:4 * HT, :]).then_inc(rows_in, 16)
            act.dma_start(rows[0:2 * HT, 3, :], cw0[4 * HT:6 * HT, :]).then_inc(rows_in, 16)
            act.dma_start(rows[2 * HT:4 * HT, 3, :], cb0).then_inc(rows_in, 16)
            act.dma_start(cvec[:, 0:FT], c[0].rearrange("(p t) -> p t", t=FT)).then_inc(c_in, 16)
            act.dma_start(cvec[:, FT:2 * FT], c_ctx.rearrange("(p t) -> p t", t=FT)).then_inc(c_in, 16)
            for hf in range(2):
                act.dma_start(x_tok[:, hf * TT // 2:(hf + 1) * TT // 2, :],
                              x[0, hf * NT // 2:(hf + 1) * NT // 2, :].rearrange("(t p) n -> p t n", p=P)
                              ).then_inc(x_in[hf], 16)
            act.dma_start(c_tok[:, :, :], ctx[0].rearrange("(t p) n -> p t n", p=P)).then_inc(ctx_in, 16)
            act.dma_start(gains[:, 0, :], q_gain.to_broadcast((P, HD))).then_inc(gain_in, 16)
            act.dma_start(gains[:, 1, :], k_gain.to_broadcast((P, HD))).then_inc(gain_in, 16)
            act.dma_start(cosT[:, :, :], rope_cos.rearrange("(t p) d -> p t d", p=P)).then_inc(rope_in, 16)
            act.dma_start(sinT[:, :, :], rope_sin.rearrange("(t p) d -> p t d", p=P)).then_inc(rope_in, 16)
            act.wait_ge(c_in, 32)
            act.activation(csil[:, :], cvec[:, :], ACT.Silu).then_inc(csil_ready, 1)

            def tok(t):
                return x_tok[:, t, :] if t < TT else c_tok[:, t - TT, :]

            act.wait_ge(cst_init, 2)
            for t in range(KT):
                if t % (TT // 2) == 0:
                    act.wait_ge(x_in[t * 2 // TT] if t < TT else ctx_in, 16)
                if t >= 1:
                    act.wait_ge(x_sq, t)
                act.activation(junk[:, :], tok(t), ACT.Square, accum_out=ss[:, t:t + 1]).then_inc(x_sq, 1)
            act.wait_ge(x_sq, KT)
            act.activation(std[:, :], ss[:, :], ACT.Sqrt, bias=eps[:, :], scale=1.0 / D).then_inc(x_sq, 1)
            act.wait_ge(x_rstd, 1)
            for t in range(KT):
                act.activation(tok(t), tok(t), ACT.Copy, scale=rstd[:, t:t + 1]).then_inc(x_scaled, 1)
            for n_ in range(3 * FT):
                f, part = n_ % FT, n_ // FT
                w = HALF if part < 2 else NC
                if n_ == 0:
                    act.wait_ge(mod_ready, 1)
                act.wait_ge(xt_ready, n_ + 1)
                if n_ >= 2:
                    act.wait_ge(h_split, n_ - 1)
                A_, S_ = (nA[0], mod[0]) if part < 2 else (nA[1], modc)
                act.activation(t0[n_ % 2][:, 0:w], ps[:, n_ % 6, 0:w], ACT.Identity,
                               bias=S_[:, f:f + 1], scale=A_[:, f:f + 1]).then_inc(t_ready, 1)

            kq, vb = 0, 0
            for b, (u, p) in enumerate(BLKS):
                act.wait_ge(blk, b + 1)
                src = ps[:, b % 4, :].rearrange("p (a n) -> p a n", a=2)
                if u == U_V:
                    if vb == 0:
                        act.wait_ge(roped, kq)
                    act.activation(v_hl[:, 2 * p:2 * p + 2, :, 0:HD], heads(src), ACT.Copy).then_inc(v_hi_ready, 1)
                    vb += 1
                    continue
                dst = k_tok[:, 2 * p:2 * p + 2, :] if u == U_K else q_tok[:, 2 * p:2 * p + 2, (u - U_Q) * UC:(u - U_Q + 1) * UC]
                act.activation(dst, src, ACT.Copy).then_inc(astep, 1)
                if kq >= 1:
                    act.wait_ge(roped, kq)
                else:
                    act.wait_ge(h_split, 3 * FT)
                act.activation(s1[:, :], ps[:, b % 4, :], ACT.Square).then_inc(kq_out, 1)
                act.wait_ge(ssq_ready, kq + 1)
                act.activation(std[:, 0:8], ss[:, 0:8], ACT.Sqrt, bias=eps[:, :], scale=1.0 / HD).then_inc(kq_std, 1)
                kq += 1

            def k_copy(j):
                act.wait_ge(kT_ready, j + 1)
                if j >= 2:
                    act.wait_ge(s_ps, (j - 1) * GQ * KT)
                act.activation(ka[j % 2][0:HD, :], wide(5, 3)[0:HD, 0:NK], ACT.Copy).then_inc(k_hi_ready, 1)
                act.wait_ge(k_hi_ready, 2 * j + 1)
                act.activation(kb[j % 2][0:HD, :], ka[j % 2][0:HD, :].bitcast(fp32), ACT.Copy).then_inc(k_hi_ready, 1)

            def q_copy(h):
                act.wait_ge(qT_ready, h + 1)
                if h >= 2:
                    act.wait_ge(s_ps, (h - 1) * KT)
                act.activation(qa[h % 2][0:HD, :], wide(6)[0:HD, :], ACT.Copy).then_inc(q_hi_ready, 1)
                act.wait_ge(q_hi_ready, 2 * h + 1)
                act.activation(qa[h % 2][HD:2 * HD, :], qa[h % 2][0:HD, :].bitcast(fp32), ACT.Copy).then_inc(q_hi_ready, 1)

            def mrow(h):
                act.wait_ge(mrow_ps, h + 1)
                act.activation(qb[h % 2][HD:HD + 1, :], wide(6)[0:1, :], ACT.Copy).then_inc(mrow_ready, 1)

            def exps(s):
                act.wait_ge(s_ps, 2 * s + 2)
                if s >= 2:
                    act.wait_ge(plo_ready, s - 1)
                    act.wait_ge(plo2_ready, s - 1)
                b = 2 * (s % 2)
                act.activation(p32[s % 2][:, :], wide(b), ACT.Exp, scale=SCALE).then_inc(p_ready, 1)

            def o_copy(n_):
                act.wait_ge(pv_step, (n_ + 1) * (KT // 2))
                if n_ >= 2:
                    act.wait_ge(o_turned, n_ - 1)
                act.activation(o_t[n_ % 2][0:HD + 1, :], ps[0:HD + 1, 4, :], ACT.Copy).then_inc(o_copied, 1)

            act.wait_ge(roped, len(KQ))
            k_copy(0); q_copy(0); mrow(0)
            exps(0); exps(1)
            q_copy(1)
            for s in range(NH * NS):
                h, e = divmod(s, NS)
                if s % HS == 0 and s > 0:
                    o_copy(s // HS - 1)
                if s > 0 and new_k(s - 1) is not None:
                    k_copy(new_k(s - 1))
                if e == NS - 1 and h + 2 < NH:
                    q_copy(h + 2)
                if s + 2 < NH * NS:
                    exps(s + 2)
                if e == ROW and h + 1 < NH:
                    mrow(h + 1)
            o_copy(2 * NH - 1)

            for n_ in range(2 * FT):
                f, hf = n_ // 2, n_ % 2
                act.wait_ge(oT_ps, n_ + 1)
                act.activation(h_hi[:, f, hf * HALF:(hf + 1) * HALF], ps[:, n_ % 4, :], ACT.Copy).then_inc(oT_hi, 1)
            for n_ in range(2 * FT):
                f, hf = n_ % FT, n_ // FT
                act.wait_ge(xr_ps, n_ + 1)
                act.activation(xT[:, f, hf * HALF:(hf + 1) * HALF], ps[:, 4 + n_ % 2, :], ACT.Copy).then_inc(xr_out, 1)

            def norm_sums(k):
                for f in range(FT):
                    n_ = k * FT + f
                    if n_ >= 4:
                        act.wait_ge(sq_used, n_ - 3)
                    act.activation(sq[f % 4][:, :], xT[:, f, :], ACT.Square).then_inc(sq_ready, 1)
                act.wait_ge(sq_used, (k + 1) * FT)
                act.activation(std[:, 0:TT], ps[:, 4, 0:TT], ACT.Sqrt, bias=eps[:, :], scale=1.0 / D).then_inc(ss_std, 1)

            def norm_hi(k, S_, c0):
                for f in range(FT):
                    act.wait_ge(nt_ready, k * FT + f + 1)
                    act.activation(h_hi[:, f, :], t_buf[f % 2][:, :], ACT.Identity,
                                   bias=S_[:, c0 + f:c0 + f + 1]).then_inc(n_hi, 1)

            def ffn(l):
                ub, hb, db = 4 * NI * l, 2 * NI * l, 16 * NI * l

                def y(j, gate, i):
                    n_ = i * 4 + (ub + 2 * gate + j)
                    act.wait_ge(up_ps, n_ + 1)
                    if gate:
                        act.wait_ge(g_lo_ready, i * 2 + (hb + j - 1) if not (isinstance(i, int) and i == 0) else max(hb, 1)) \
                            if not (isinstance(i, int) and i == 0 and l == 0) else None
                    elif not (isinstance(i, int) and i == 0 and l == 0):
                        act.wait_ge(g_ready, i * 2 + (hb + j - 1))
                    t = (y_gate if gate else y_val)[j]
                    q = HT * gate + j
                    act.activation(t[:, :], wide(2 * j), ACT.Identity,
                                   bias=cst[:, bass.ds(i * 2 + (CV_B + q), 1)],
                                   scale=cst[:, bass.ds(i * 2 + (CV_W[1] + q), 1)]).then_inc(y_ready, 1)

                def step(i):
                    for j in range(2):
                        y(j, 0, i)
                    for j in range(2):
                        y(j, 1, i)
                    for j in range(2):
                        act.wait_ge(cv_done, i * 4 + (ub + 2 + j + 1))
                        act.activation(y_gate[j][:, :], y_gate[j][:, :], ACT.Silu).then_inc(silu_ready, 1)
                    for j in range(2):
                        act.wait_ge(g_ready, i * 2 + (hb + j + 1))
                        if not (isinstance(i, int) and i == 0 and l == 0):
                            act.wait_ge(dn_ps, i * 16 + db)
                        act.activation(g_hi[:, j, :], y_gate[j][:, :], ACT.Copy).then_inc(g_hi_ready, 1)

                step(0)
                with act.Fori(1, NI) as i:
                    step(i)

            act.wait_ge(wo_out, NG)
            act.wait_ge(ada_sum, 2 * NU)
            norm_sums(0)
            norm_hi(0, mod[0], 3 * FT)
            act.wait_ge(n_lo, FT)
            ffn(0)
            cw1 = conv_w[1].rearrange("k (j p) -> (k j) p", p=P)
            cb1 = conv_b[1].rearrange("(j p) -> j p", p=P)
            act.wait_ge(dn_out, 16 * NI)
            r1 = t_buf[0][:, :].rearrange("p (a n) -> p a n", n=P)
            act.dma_start(r1[0:4 * HT, 0, :], cw1[0:4 * HT, :]).then_inc(conv1_in, 16)
            act.dma_start(r1[0:2 * HT, 1, :], cw1[4 * HT:6 * HT, :]).then_inc(conv1_in, 16)
            act.dma_start(r1[2 * HT:4 * HT, 1, :], cb1).then_inc(conv1_in, 16)
            act.dma_start(edge[:, :], pool_edge.rearrange("(a n) -> a n", a=1).to_broadcast((P, 4 * 2 * PAD))).then_inc(edge_in, 16)
            norm_sums(1)
            for f in range(FT):
                act.wait_ge(nt_ready, FT + f + 1)
                act.activation(hp[:, PAD:PAD + NT], t_buf[f % 2][:, :], ACT.Identity,
                               bias=mod[1][:, f:f + 1]).then_inc(hp_ready, 1)
                act.wait_ge(pooled, f + 1)
                act.activation(h_hi[:, f, :], win[0][:, 0:NT], ACT.Copy).then_inc(n_hi, 1)
            for n_ in range(2 * FT):
                act.wait_ge(pl_ps, n_ + 1)
                if n_ >= 2:
                    act.wait_ge(pl_out, n_ - 1)
                f = n_ // 2
                act.activation(t_buf[n_ % 2][:, 0:HALF], ps[:, n_ % 4, :], ACT.Identity,
                               bias=gb[:, f:f + 1], scale=gs[:, f:f + 1]).then_inc(pl_t, 1)
            act.wait_ge(pl_out, 2 * FT)
            norm_sums(2)
            norm_hi(2, mod[1], 3 * FT)
            act.wait_ge(n_lo, 3 * FT)
            ffn(1)
            act.wait_ge(dn_out, 32 * NI)
            norm_sums(3)
            for f in range(FT):
                act.activation(xT[:, f, :], xT[:, f, :], ACT.Copy, scale=cst[:, C_FN + f:C_FN + f + 1]).then_inc(fin_scaled, 1)
            for t in range(TT):
                act.wait_ge(fin_ps, t + 1)
                if t == 0:
                    act.wait_ge(ss_rstd, 4)
                if t >= 2:
                    act.wait_ge(out_done[t % 2], 16 * (t // 2))
                act.activation(o_sb[t % 2][:, :], wide(2 * (t % 2)), ACT.Copy, scale=rstd[:, t:t + 1]).then_inc(fin_out, 1)

        @block.vector
        def _(dve):
            chain = [0]

            def link(ins):
                chain[0] += 1
                ins.then_inc(vstep, 1)
                dve.wait_ge(vstep, chain[0])

            dve.memset(one[:, :], 1.0).then_inc(cst_init, 1)
            dve.memset(eps[:, :], EPS).then_inc(cst_init, 1)
            dve.wait_ge(rows_t, 1)
            dve.tensor_copy(cst[:, :], ps[:, 6, 0:2 * MT + 7 * FT + NCONV]).then_inc(cst_ready, 1)

            def ada(u):
                dve.wait_ge(ada_in[u % 2], 16 * (u // 2 + 1))
                if u >= 2:
                    dve.wait_ge(ada_sum, u - 1)
                if u == 0:
                    dve.wait_ge(csil_ready, 1)
                w = ada_raw[u % 2]
                vecs = [(acc[u % 2], 0)] + ([(accc[u % 2], FT)] if u < EARLY else [])
                for t in range(FT):
                    for a, c0 in vecs:
                        s_ = csil[:, c0 + t:c0 + t + 1]
                        if t == 0:
                            ins = dve.tensor_scalar(a[:, :], w[:, t, :], s_, None, ALU.mult)
                        else:
                            ins = dve.scalar_tensor_tensor(out=a[:, :], in0=w[:, t, :], scalar=s_,
                                                           in1=a[:, :], op0=ALU.mult, op1=ALU.add)
                        if t < FT - 1:
                            ins.then_inc(vstep, 1)
                            chain[0] += 1
                    if t < FT - 1:
                        dve.wait_ge(vstep, chain[0])
                ins.then_inc(ada_acc, 1)

            def norm_gain(dst, w0, scale):
                return dve.scalar_tensor_tensor(out=dst[:, :], in0=scale, scalar=1.0,
                                                in1=cst[:, C_NW + w0 * FT:C_NW + (w0 + 1) * FT],
                                                op0=ALU.add, op1=ALU.mult)

            for u in range(EARLY):
                ada(u)
                if u == 3:
                    dve.wait_ge(x_sq, KT + 1)
                    dve.reciprocal(rstd[:, :], std[:, :]).then_inc(x_rstd, 1)
            dve.wait_ge(gain_in, 32)
            dve.wait_ge(rope_in, 32)
            for n_ in range(2):
                g = gains[:, n_:n_ + 1, :]
                dve.tensor_tensor(tabs[2 * n_][:, :, :], cosT[:, :, :], g.to_broadcast((P, TT, HD)), ALU.mult)
                for r in range(2):
                    for s_ in range(2):
                        o0, i0 = 32 * r + 16 * s_, 32 * r + 16 * (1 - s_)
                        ins = dve.tensor_tensor(tabs[2 * n_ + 1][:, :, o0:o0 + 16], sinT[:, :, o0:o0 + 16],
                                                gains[:, n_:n_ + 1, i0:i0 + 16].to_broadcast((P, TT, 16)), ALU.mult)
            ins.then_inc(tab_ready, 1)
            dve.wait_ge(ada_sum, EARLY)
            dve.wait_ge(cst_ready, 1)
            dve.tensor_tensor(mod[0][:, 0:2 * FT], ps[:, 7, 0:2 * FT], cst[:, 0:2 * FT], ALU.add)
            link(dve.tensor_tensor(modc[:, :], ps[:, 7, MT:MT + 2 * FT], cst[:, 0:2 * FT], ALU.add))
            norm_gain(nA[0], 0, mod[0][:, FT:2 * FT])
            norm_gain(nA[1], 0, modc[:, FT:2 * FT]).then_inc(mod_ready, 1)

            for n_ in range(3 * FT):
                f, part = n_ % FT, n_ // FT
                w = HALF if part < 2 else NC
                hi = h_hi[:, f, part * HALF:part * HALF + w] if part < 2 else ch_hi[:, f, :]
                lo = h_lo[:, f, part * HALF:part * HALF + w] if part < 2 else ch_lo[:, f, :]
                dve.wait_ge(t_ready, n_ + 1)
                if n_ == 2 * FT:
                    dve.wait_ge(xt_ready, 2 * FT)
                link(dve.tensor_copy(hi, t0[n_ % 2][:, 0:w]))
                dve.tensor_tensor(lo, t0[n_ % 2][:, 0:w], hi.bitcast(fp32), ALU.subtract).then_inc(h_split, 1)

            dve.wait_ge(tab_ready, 1)
            kq, vb = 0, 0
            for b, (u, p) in enumerate(BLKS):
                if u == U_V:
                    if vb == 0:
                        dve.memset(v_hl[:, :, :, HD:HD + 2].bitcast(fp32), 1.0)
                    dve.wait_ge(v_hi_ready, vb + 1)
                    dve.tensor_tensor(v_hl[:, 2 * p:2 * p + 2, :, HD + 2:VW],
                                      heads(ps[:, b % 4, :].rearrange("p (a n) -> p a n", a=2)),
                                      v_hl[:, 2 * p:2 * p + 2, :, 0:HD].bitcast(fp32), ALU.subtract).then_inc(v_out, 1)
                    vb += 1
                else:
                    dst = k_tok[:, 2 * p:2 * p + 2, :] if u == U_K else q_tok[:, 2 * p:2 * p + 2, (u - U_Q) * UC:(u - U_Q + 1) * UC]
                    s1h = s1[:, :].rearrange("p (a d) -> p a d", d=HD)
                    dve.wait_ge(kq_out, kq + 1)
                    dve.tensor_reduce(ss[:, 0:8], s1h, AX.X, ALU.add).then_inc(ssq_ready, 1)
                    dve.wait_ge(kq_std, kq + 1)
                    link(dve.reciprocal(rstd[:, 0:8], std[:, 0:8]))
                    dh = heads(dst)
                    link(dve.tensor_tensor(dh, dh, rstd[:, 0:8].rearrange("p (a h o) -> p a h o", a=2, o=1)
                                           .to_broadcast((P, 2, 4, HD)), ALU.mult))
                    if u == U_K and p == NP_:
                        dve.tensor_tensor(dst.rearrange("p a (h d) -> p (a h) d", d=HD),
                                          dst.rearrange("p a (h d) -> p (a h) d", d=HD),
                                          gains[:, 1:2, :].to_broadcast((P, 8, HD)), ALU.mult).then_inc(roped, 1)
                    else:
                        cos, sin = (tabs[2], tabs[3]) if u == U_K else (tabs[0], tabs[1])
                        s1q = s1[:, :].rearrange("p (a h d) -> p a h d", a=2, d=HD)
                        dve.tensor_tensor(s1q, dh, cos[:, 2 * p:2 * p + 2, :].rearrange("p a (o d) -> p a o d", o=1)
                                          .to_broadcast((P, 2, 4, HD)), ALU.mult)
                        for a in range(2):
                            for s_ in range(2):
                                sv = s2[:, a * 256:(a + 1) * 256].rearrange("p (h r s i) -> p h r s i", h=4, r=2, s=2)
                                dv = dst[:, a, :].rearrange("p (h r s i) -> p h r s i", h=4, r=2, s=2)
                                tv = sin[:, 2 * p + a, :].rearrange("p (o r s i) -> p o r s i", o=1, r=2, s=2)
                                ins = dve.tensor_tensor(sv[:, :, :, s_, :], dv[:, :, :, 1 - s_, :],
                                                        tv[:, :, :, s_, :].to_broadcast((P, 4, 2, 16)), ALU.mult)
                        link(ins)
                        dve.tensor_tensor(dst, s1[:, :].rearrange("p (a n) -> p a n", a=2),
                                          s2[:, :].rearrange("p (a n) -> p a n", a=2), ALU.add).then_inc(roped, 1)
                    kq += 1
                if b in ADA_AT:
                    ada(ADA_AT[b])
            dve.wait_ge(ada_sum, NU)
            link(dve.tensor_tensor(mod[0][:, 2 * FT:MT], ps[:, 7, 2 * FT:MT], cst[:, 2 * FT:MT], ALU.add))
            norm_gain(nA[2], 1, mod[0][:, 4 * FT:5 * FT]).then_inc(mod_ready, 1)

            dve.wait_ge(id_ready, 2)
            dve.tensor_copy(id_r[:, :], ident[:, :])
            for i in range(2):
                ins = dve.memset(kb[i][HD:HD + 1, :].bitcast(fp32), 1.0)
            ins.then_inc(id_ready, 1)

            def k_lo(j):
                dve.wait_ge(k_hi_ready, 2 * j + 1)
                dve.tensor_tensor(ka[j % 2][HD:2 * HD, :], wide(5, 3)[0:HD, 0:NK],
                                  ka[j % 2][0:HD, :].bitcast(fp32), ALU.subtract).then_inc(k_lo_ready, 1)

            def q_lo(h):
                dve.wait_ge(q_hi_ready, 2 * h + 1)
                dve.tensor_tensor(qb[h % 2][0:HD, :], wide(6)[0:HD, :],
                                  qa[h % 2][0:HD, :].bitcast(fp32), ALU.subtract).then_inc(q_lo_ready, 1)

            def maxes(h, n_):
                t, piece = divmod(n_, 3)
                w = min(HALF, NK - piece * HALF)
                g = h * 3 * TT + n_
                dve.wait_ge(mx_ps, g + 1)
                dve.tensor_reduce(mx[h % 2][:, n_:n_ + 1], ps[:, 6 + g % 2, 0:w], AX.X, ALU.max).then_inc(mx_red, 1)

            def neg_max(h):
                dve.wait_ge(mx_red, (h + 1) * 3 * TT)
                link(dve.tensor_reduce(mxr[:, :], mx[h % 2][:, :].rearrange("p (t k) -> p t k", k=3), AX.X, ALU.max))
                dve.tensor_scalar(mneg[h % 2][:, :], mxr[:, :], -1.0, None, ALU.mult).then_inc(mneg_ready, 1)

            def p_low(s):
                dve.wait_ge(phi_ready, s + 1)
                dve.tensor_tensor(p_lo[s % 3][:, 0:LC], p32[s % 2][:, 0:LC], p_hi[s % 3][:, 0:LC].bitcast(fp32),
                                  ALU.subtract).then_inc(plo_ready, 1)

            def o_norm(n_):
                h, hf = divmod(n_, 2)
                dve.wait_ge(o_turned, n_ + 1)
                src = ps[:, 5, 0:4 * (HD + 2)].rearrange("p (t d) -> p t d", d=HD + 2)
                link(dve.reciprocal(rden[:, :].rearrange("p (t o) -> p t o", o=1), src[:, :, HD:HD + 1]))
                dve.tensor_tensor(q_tok[:, 4 * hf:4 * hf + 4, h * HD:(h + 1) * HD], src[:, :, 0:HD],
                                  rden[:, :].rearrange("p (t o) -> p t o", o=1).to_broadcast((P, 4, HD)),
                                  ALU.mult).then_inc(o_ready, 1)

            k_lo(0); q_lo(0)
            for n_ in range(NM):
                maxes(0, n_)
            neg_max(0)
            p_low(0)
            q_lo(1)
            for n_ in range(3):
                maxes(1, n_)
            for s in range(NH * NS):
                h, e = divmod(s, NS)
                if s > 0 and new_k(s - 1) is not None:
                    k_lo(new_k(s - 1))
                if e == NS - 1 and h + 2 < NH:
                    q_lo(h + 2)
                g, ns = pieces(s)
                for n_ in ns[0:1]:
                    maxes(g, n_)
                if s + 1 < NH * NS:
                    p_low(s + 1)
                for n_ in ns[1:3]:
                    maxes(g, n_)
                if ns and ns[-1] == NM - 1:
                    neg_max(g)
                if s % HS == 1 and s > HS:
                    o_norm(s // HS - 1)
            o_norm(2 * NH - 1)

            for n_ in range(2 * FT):
                f, hf = n_ // 2, n_ % 2
                dve.wait_ge(oT_hi, n_ + 1)
                dve.tensor_tensor(h_lo[:, f, hf * HALF:(hf + 1) * HALF], ps[:, n_ % 4, :],
                                  h_hi[:, f, hf * HALF:(hf + 1) * HALF].bitcast(fp32), ALU.subtract).then_inc(oT_lo, 1)
            for g in range(NG):
                f, hf = g // 2, g % 2
                dve.wait_ge(wo_ps, g + 1)
                if g == 0:
                    dve.wait_ge(xr_out, 2 * FT)
                xs = xT[:, f, hf * HALF:(hf + 1) * HALF]
                dve.scalar_tensor_tensor(out=xs, in0=ps[:, g % 4, :], scalar=mod[0][:, 2 * FT + f:2 * FT + f + 1],
                                         in1=xs, op0=ALU.mult, op1=ALU.add).then_inc(wo_out, 1)
                for u in WO_ADA[g]:
                    ada(u)
            dve.wait_ge(ada_sum, 2 * NU)
            link(dve.tensor_tensor(mod[1][:, :], ps[:, 7, 0:MT], cst[:, MT:2 * MT], ALU.add))
            norm_gain(nA[3], 2, mod[1][:, FT:2 * FT])
            norm_gain(nA[4], 3, mod[1][:, 4 * FT:5 * FT])
            link(dve.tensor_tensor(gs[:, :], mod[1][:, 2 * FT:3 * FT], cst[:, C_PS:C_PS + FT], ALU.mult))
            dve.tensor_tensor(gb[:, :], gs[:, :], cst[:, C_PB:C_PB + FT], ALU.mult).then_inc(mod_ready, 1)

            def norm_rstd(k):
                dve.wait_ge(ss_std, k + 1)
                dve.reciprocal(rstd[:, 0:TT], std[:, 0:TT]).then_inc(ss_rstd, 1)

            def norm_t(k, f, A_):
                if f == 0:
                    dve.wait_ge(bc_ready, k + 1)
                if f >= 2:
                    dve.wait_ge(hp_ready if k == 1 else n_lo, f - 1 if k == 1 else k * FT + f - 1)
                dve.scalar_tensor_tensor(out=t_buf[f % 2][:, :], in0=xT[:, f, :], scalar=A_[:, f:f + 1],
                                         in1=wide(6), op0=ALU.mult, op1=ALU.mult).then_inc(nt_ready, 1)

            def norm_split(k, A_, S_, c0):
                norm_rstd(k)
                norm_t(k, 0, A_)
                for f in range(FT):
                    if f + 1 < FT:
                        norm_t(k, f + 1, A_)
                    dve.wait_ge(n_hi, k * FT + f + 1)
                    dve.scalar_tensor_tensor(out=h_lo[:, f, :], in0=t_buf[f % 2][:, :], scalar=S_[:, c0 + f:c0 + f + 1],
                                             in1=h_hi[:, f, :].bitcast(fp32), op0=ALU.add, op1=ALU.subtract).then_inc(n_lo, 1)

            def ffn(l):
                ub, hb, db = 4 * NI * l, 2 * NI * l, 16 * NI * l
                g2 = mod[l][:, 5 * FT:6 * FT]

                def conv(j, gate, i):
                    n_ = i * 4 + (ub + 2 * gate + j)
                    q = HT * gate + j
                    t = (y_gate if gate else y_val)[j]
                    up = wide(2 * j)
                    dve.wait_ge(y_ready, n_ + 1)
                    dve.scalar_tensor_tensor(out=t[:, 1:NT], in0=up[:, 0:NT - 1],
                                             scalar=cst[:, bass.ds(i * 2 + (CV_W[0] + q), 1)],
                                             in1=t[:, 1:NT], op0=ALU.mult, op1=ALU.add).then_inc(cv_half, 1)
                    dve.wait_ge(cv_half, n_ + 1)
                    dve.scalar_tensor_tensor(out=t[:, 0:NT - 1], in0=up[:, 1:NT],
                                             scalar=cst[:, bass.ds(i * 2 + (CV_W[2] + q), 1)],
                                             in1=t[:, 0:NT - 1], op0=ALU.mult, op1=ALU.add).then_inc(cv_done, 1)

                def down(i):
                    for n_ in range(16):
                        f, hf = n_ // 2, n_ % 2
                        xs = xT[:, f, hf * HALF:(hf + 1) * HALF]
                        dve.wait_ge(dn_ps, i * 16 + (db + n_ + 1))
                        dve.scalar_tensor_tensor(out=xs, in0=ps[:, 4 + n_ % 4, :], scalar=g2[:, f:f + 1],
                                                 in1=xs, op0=ALU.mult, op1=ALU.add).then_inc(dn_out, 1)

                def gated(i):
                    for j in range(2):
                        dve.wait_ge(silu_ready, i * 2 + (hb + j + 1))
                        dve.tensor_tensor(y_gate[j][:, :], y_gate[j][:, :], y_val[j][:, :], ALU.mult).then_inc(g_ready, 1)
                    for j in range(2):
                        dve.wait_ge(g_hi_ready, i * 2 + (hb + j + 1))
                        dve.tensor_tensor(g_lo[:, j, :], y_gate[j][:, :], g_hi[:, j, :].bitcast(fp32),
                                          ALU.subtract).then_inc(g_lo_ready, 1)

                conv(0, 0, 0); conv(1, 0, 0); conv(0, 1, 0); conv(1, 1, 0)
                gated(0)
                with dve.Fori(1, NI) as i:
                    conv(0, 0, i); conv(1, 0, i)
                    down(i - 1)
                    conv(0, 1, i); conv(1, 1, i)
                    gated(i)
                down(NI - 1)

            dve.wait_ge(wo_out, NG)
            norm_split(0, nA[2], mod[0], 3 * FT)
            ffn(0)
            dve.wait_ge(rows_t, 2)
            dve.tensor_copy(cst[:, C_CV:C_CV + NCONV], ps[:, 5, 0:NCONV]).then_inc(cst_ready, 1)

            norm_rstd(1)
            dve.wait_ge(edge_in, 16)
            dve.wait_ge(sq_used, 2 * FT)
            dve.memset(hp[:, 0:PAD], 0.0)
            link(dve.memset(hp[:, PAD + NT:PW], 0.0))
            norm_t(1, 0, nA[3])
            for f in range(FT):
                if f + 1 < FT:
                    norm_t(1, f + 1, nA[3])
                g = f * 4 // FT
                W = WINDOWS[g]
                dve.wait_ge(hp_ready, f + 1)
                if f >= 1:
                    dve.wait_ge(n_lo, FT + f)
                    dve.wait_ge(n_hi, FT + f)
                m = W // 2 - 1
                src, d = hp, 0
                link(dve.tensor_tensor(win[g % 2][:, PAD - m:PAD + NT + m], hp[:, PAD - m - 1:PAD + NT + m - 1],
                                       hp[:, PAD - m:PAD + NT + m], ALU.add))
                for lev in range(1, g + 1):
                    r = 2 ** (lev - 1)
                    m -= r
                    src, dst = win[(g - lev + 1) % 2], win[(g - lev) % 2]
                    link(dve.tensor_tensor(dst[:, PAD - m:PAD + NT + m], src[:, PAD - m - r:PAD + NT + m - r],
                                           src[:, PAD - m + r:PAD + NT + m + r], ALU.add))
                w0 = win[0]
                E0 = edge[:, 2 * g * PAD:2 * g * PAD + W // 2]
                E1 = edge[:, (2 * g + 1) * PAD:(2 * g + 1) * PAD + W // 2]
                dve.tensor_tensor(w0[:, PAD:PAD + W // 2], w0[:, PAD:PAD + W // 2], E0, ALU.mult)
                link(dve.tensor_tensor(w0[:, PAD + NT - W // 2:PAD + NT], w0[:, PAD + NT - W // 2:PAD + NT], E1, ALU.mult))
                link(dve.scalar_tensor_tensor(out=win[1][:, 0:NT], in0=w0[:, PAD:PAD + NT], scalar=1.0 / W,
                                              in1=hp[:, PAD:PAD + NT], op0=ALU.mult, op1=ALU.subtract))
                dve.tensor_copy(win[0][:, 0:NT], win[1][:, 0:NT]).then_inc(pooled, 1)
                dve.wait_ge(n_hi, FT + f + 1)
                dve.tensor_tensor(h_lo[:, f, :], win[1][:, 0:NT], h_hi[:, f, :].bitcast(fp32), ALU.subtract).then_inc(n_lo, 1)
            for n_ in range(2 * FT):
                f, hf = n_ // 2, n_ % 2
                xs = xT[:, f, hf * HALF:(hf + 1) * HALF]
                dve.wait_ge(pl_t, n_ + 1)
                dve.tensor_tensor(xs, xs, t_buf[n_ % 2][:, 0:HALF], ALU.add).then_inc(pl_out, 1)
            norm_split(2, nA[4], mod[1], 3 * FT)
            ffn(1)
            norm_rstd(3)

        @block.tensor
        def _(pe):
            def product(dst, terms, first=True, last=True):
                n_ = len(terms)
                for k, (ah, al, bh, bl) in enumerate(terms):
                    pe.matmul(dst, ah, bh, start=(k == 0 and first), stop=False)
                    pe.matmul(dst, ah, bl, start=False, stop=False)
                    mm = pe.matmul(dst, al, bh, start=False, stop=(k == n_ - 1 and last))
                return mm

            pe.wait_ge(rows_in, 16 * 8)
            pe.wait_ge(id_ready, 2)
            pe.transpose(ps[:, 6, 0:2 * MT], rows[0:2 * MT, 0, :], ident[0:2 * MT, 0:2 * MT])
            pe.transpose(ps[:, 6, 2 * MT:2 * MT + 7 * FT], rows[0:7 * FT, 1, :], ident[0:7 * FT, 0:7 * FT])
            pe.transpose(ps[:, 6, C_CV:C_CV + 4 * HT], rows[0:4 * HT, 2, :], ident[0:4 * HT, 0:4 * HT])
            pe.transpose(ps[:, 6, C_CV + 4 * HT:C_CV + 8 * HT], rows[0:4 * HT, 3, :], ident[0:4 * HT, 0:4 * HT]).then_inc(rows_t, 1)

            def ada(u):
                pe.wait_ge(ada_acc, u + 1)
                if u == 0:
                    pe.wait_ge(cst_init, 2)
                if u == EARLY:
                    pe.wait_ge(mod_ready, 1)
                if u == NU:
                    pe.wait_ge(mod_ready, 2)
                v = u % NU
                for j in range(UC // P):
                    if u < EARLY:
                        pe.matmul(ps[:, 7, MT + 2 * v + j:MT + 2 * v + j + 1], accc[u % 2][:, j * P:(j + 1) * P],
                                  one[:, :], start=True, stop=True)
                    mm = pe.matmul(ps[:, 7, 2 * v + j:2 * v + j + 1], acc[u % 2][:, j * P:(j + 1) * P],
                                   one[:, :], start=True, stop=True)
                mm.then_inc(ada_sum, 1)

            for u in range(EARLY):
                ada(u)
            for n_ in range(3 * FT):
                f, part = n_ % FT, n_ // FT
                if n_ == 0:
                    pe.wait_ge(cst_ready, 1)
                if n_ % FT == 0:
                    pe.wait_ge(x_scaled, TT // 2 * (part + 1) if part < 2 else KT)
                if n_ >= 6:
                    pe.wait_ge(t_ready, n_ - 5)
                for t in range(TT // 2 if part < 2 else CT):
                    src = x_tok[:, part * TT // 2 + t, f * P:(f + 1) * P] if part < 2 else c_tok[:, t, f * P:(f + 1) * P]
                    mm = pe.transpose(ps[:, n_ % 6, t * P:(t + 1) * P], src, ident[:, :])
                mm.then_inc(xt_ready, 1)

            for b, (u, p) in enumerate(BLKS):
                if u < U_WO and (b == 0 or BLKS[b - 1][0] != u):
                    pe.wait_ge(w_split, u + 1)
                if u == U_K:
                    pe.wait_ge(h_split, FT * (p // (NP_ // 2) + 1))
                if b < 4:
                    pe.wait_ge(t_ready, 3 * FT) if p == NP_ else pe.wait_ge(t_ready, 2 * FT + b % 4 + 5 - (0 if b else 0)) if False else pe.wait_ge(t_ready, 3 * FT)
                else:
                    c_ = b - 4
                    if BLKS[c_][0] == U_V:
                        pe.wait_ge(v_out, VB.index(c_) + 1)
                    else:
                        pe.wait_ge(kq_out, KQ.index(c_) + 1)
                bh, bl = hl(SLOT[u])
                for a in range(2):
                    t = 2 * p + a
                    if p < NP_:
                        terms = [(h_hi[:, k, t * P:(t + 1) * P], h_lo[:, k, t * P:(t + 1) * P], bh[:, k, :], bl[:, k, :]) for k in range(FT)]
                    else:
                        terms = [(ch_hi[:, k, a * P:(a + 1) * P], ch_lo[:, k, a * P:(a + 1) * P], bh[:, k, :], bl[:, k, :]) for k in range(FT)]
                    mm = product(ps[:, b % 4, a * UC:(a + 1) * UC], terms)
                mm.then_inc(blk, 1)
                if b - 2 in ADA_AT:
                    ada(ADA_AT[b - 2])

            def turn_k(j):
                for t in range(KT):
                    mm = pe.transpose(wide(5, 3)[0:HD, t * P:(t + 1) * P], k_tok[:, t, j * HD:(j + 1) * HD], ident[:, :])
                mm.then_inc(kT_ready, 1)

            def turn_q(h):
                for t in range(TT):
                    mm = pe.transpose(wide(6)[0:HD, t * P:(t + 1) * P], q_tok[:, t, h * HD:(h + 1) * HD], ident[:, :])
                mm.then_inc(qT_ready, 1)

            def max_scores(h, n_):
                t, piece = divmod(n_, 3)
                w = min(HALF, NK - piece * HALF)
                g = h * NM + n_
                if n_ == 0:
                    pe.wait_ge(q_hi_ready, 2 * h + 2)
                    pe.wait_ge(q_lo_ready, h + 1)
                    pe.wait_ge(k_lo_ready, h // GQ + 1)
                if g >= 2:
                    pe.wait_ge(mx_red, g - 1)
                pe.matmul(ps[:, 6 + g % 2, 0:w], qa[h % 2][:, t * P:(t + 1) * P],
                          ka[h // GQ % 2][:, piece * HALF:piece * HALF + w], start=True, stop=True).then_inc(mx_ps, 1)

            def max_row(h):
                pe.wait_ge(mneg_ready, h + 1)
                for t in range(TT):
                    mm = pe.matmul(wide(6)[0:1, t * P:(t + 1) * P], mneg[h % 2][:, t:t + 1], id_r[:, :], start=True, stop=True)
                mm.then_inc(mrow_ps, 1)

            def scores(s, a):
                h, e = divmod(s, NS)
                hf, kp = divmod(e, HS)
                if a == 0:
                    if e == 0:
                        pe.wait_ge(mrow_ready, h + 1)
                        if h % GQ == 0:
                            pe.wait_ge(k_hi_ready, 2 * (h // GQ) + 2)
                    if s >= 2:
                        pe.wait_ge(p_ready, s - 1)
                A_, B_ = ka[h // GQ % 2], kb[h // GQ % 2]
                qs = slice(hf * HALF, (hf + 1) * HALF)
                ks = slice((2 * kp + a) * P, (2 * kp + a + 1) * P)
                dst = ps[:, 2 * (s % 2) + a, :]
                pe.matmul(dst, A_[:, ks], qa[h % 2][:, qs], start=True, stop=False)
                pe.matmul(dst, B_[0:HD + 1, ks], qb[h % 2][0:HD + 1, qs], start=False, stop=True).then_inc(s_ps, 1)

            def values(s, a):
                h, e = divmod(s, NS)
                hf, kp = divmod(e, HS)
                j = h // GQ
                if a == 0:
                    if kp == 0 and s > 0:
                        pe.wait_ge(o_copied, s // HS)
                    pe.wait_ge(plo_ready, s + 1)
                    pe.wait_ge(plo2_ready, s + 1)
                t = 2 * kp + a
                v1, v2 = v_hl[:, t, j, 0:HD + 1], v_hl[:, t, j, HD + 2:VW]
                cs = slice(a * HALF, (a + 1) * HALF)
                st = kp == 0 and a == 0
                en = kp == HS - 1 and a == 1
                pe.matmul(ps[0:HD + 1, 4, :], v1, p_hi[s % 3][:, cs], start=st, stop=False, skip_group_check=True)
                pe.matmul(ps[0:HD, 4, :], v2, p_hi[s % 3][:, cs], start=False, stop=False, skip_group_check=True)
                mm = pe.matmul(ps[0:HD + 1, 4, :], v1, p_lo[s % 3][:, cs], start=False, stop=en, skip_group_check=True)
                if a == 1:
                    mm.then_inc(pv_step, 1)

            def turn_o(n_):
                pe.wait_ge(o_copied, n_ + 1)
                if n_ >= 1:
                    pe.wait_ge(o_ready, n_)
                for t in range(4):
                    mm = pe.transpose(ps[:, 5, t * (HD + 2):t * (HD + 2) + HD + 1], o_t[n_ % 2][0:HD + 1, t * P:(t + 1) * P],
                                      ident[0:HD + 1, 0:HD + 1])
                mm.then_inc(o_turned, 1)

            pe.wait_ge(roped, len(KQ))
            pe.wait_ge(id_ready, 3)
            pe.wait_ge(mod_ready, 2)
            turn_k(0)
            pe.wait_ge(k_lo_ready, 1)
            turn_q(0)
            for n_ in range(NM):
                max_scores(0, n_)
            max_row(0)
            for s in range(2):
                scores(s, 0); scores(s, 1)
            pe.wait_ge(mrow_ready, 1)
            turn_q(1)
            for n_ in range(3):
                max_scores(1, n_)
            for s in range(NH * NS):
                h, e = divmod(s, NS)
                g, ns = pieces(s)
                if s + 2 < NH * NS:
                    scores(s + 2, 0)
                    for n_ in ns[0:1]:
                        max_scores(g, n_)
                    scores(s + 2, 1)
                if e == ROW and h + 1 < NH:
                    max_row(h + 1)
                values(s, 0)
                for n_ in ns[1:2]:
                    max_scores(g, n_)
                values(s, 1)
                for n_ in ns[2:3]:
                    max_scores(g, n_)
                if s % HS == 1 and s > HS:
                    turn_o(s // HS - 1)
                if new_k(s) is not None:
                    pe.wait_ge(mrow_ready, h + 2)
                    pe.wait_ge(o_ready, 2 * h + 1)
                    turn_k(new_k(s))
                if e == TURN_Q and h + 2 < NH:
                    pe.wait_ge(mrow_ready, h + 2)
                    if (h + 2) % GQ == 0:
                        pe.wait_ge(k_lo_ready, (h + 2) // GQ + 1)
                    turn_q(h + 2)
            turn_o(2 * NH - 1)

            for n_ in range(2 * FT):
                f, hf = n_ // 2, n_ % 2
                if n_ == 0:
                    pe.wait_ge(o_ready, 2 * NH)
                if n_ < 4:
                    pe.wait_ge(p_ready, NH * NS)
                else:
                    pe.wait_ge(oT_lo, n_ - 3)
                for t in range(4):
                    mm = pe.transpose(ps[:, n_ % 4, t * P:(t + 1) * P], q_tok[:, 4 * hf + t, f * P:(f + 1) * P], ident[:, :])
                mm.then_inc(oT_ps, 1)
            for n_ in range(2 * FT):
                f, hf = n_ % FT, n_ // FT
                if f == 0:
                    pe.wait_ge(xre_in, 16 * (hf + 1))
                if n_ >= 2:
                    pe.wait_ge(xr_out, n_ - 1)
                for t in range(4):
                    mm = pe.transpose(ps[:, 4 + n_ % 2, t * P:(t + 1) * P], x_re[:, t, f * P:(f + 1) * P], ident[:, :])
                mm.then_inc(xr_ps, 1)
            for g in range(NG):
                u, o, hf = U_WO + g // 4, g // 2 % 2, g % 2
                if g % 4 == 0:
                    pe.wait_ge(w_split, u + 1)
                if g < 4:
                    pe.wait_ge(oT_lo, 2 * FT)
                else:
                    pe.wait_ge(wo_out, g - 3)
                ah, al = hl(SLOT[u])
                cs, hs_ = slice(o * P, (o + 1) * P), slice(hf * HALF, (hf + 1) * HALF)
                product(ps[:, g % 4, :], [(ah[:, k, cs], al[:, k, cs], h_hi[:, k, hs_], h_lo[:, k, hs_]) for k in range(FT)]
                        ).then_inc(wo_ps, 1)
                if g >= 1:
                    for u_ in WO_ADA[g - 1]:
                        ada(u_)
            for u_ in WO_ADA[NG - 1]:
                ada(u_)

            def norm_sums(k):
                for f in range(FT):
                    pe.wait_ge(sq_ready, k * FT + f + 1)
                    for t in range(TT):
                        mm = pe.matmul(ps[:, 4, t:t + 1], sq[f % 4][:, t * P:(t + 1) * P], one[:, :],
                                       start=(f == 0 and t == 0), stop=(f == FT - 1), skip_group_check=True)
                    mm.then_inc(sq_used, 1)

            def norm_spread(k):
                pe.wait_ge(ss_rstd, k + 1)
                for t in range(TT):
                    mm = pe.matmul(wide(6)[:, t * P:(t + 1) * P], rstd[:, t:t + 1].to_broadcast((P, P)), ident[:, :],
                                   start=True, stop=True)
                mm.then_inc(bc_ready, 1)

            def ffn(l):
                b, ub, hb, db = FB[l], 4 * NI * l, 2 * NI * l, 16 * NI * l

                def up(gate, i, u):
                    s = gate
                    ah, al = hl(s)
                    pe.wait_ge(w_split, u + 1)
                    for j in range(2):
                        n_ = i * 4 + (ub + 2 * gate + j)
                        if not (isinstance(i, int) and i == 0 and gate == 0 and l == 0):
                            pe.wait_ge(cv_done, n_ - 1)
                        cs = slice(j * P, (j + 1) * P)
                        for hf in range(2):
                            hs_ = slice(hf * HALF, (hf + 1) * HALF)
                            mm = product(ps[:, 2 * j + hf, :], [(ah[:, k, cs], al[:, k, cs], h_hi[:, k, hs_], h_lo[:, k, hs_]) for k in range(FT)])
                        mm.then_inc(up_ps, 1)

                def down(i, u):
                    ah, al = hl_down(2)
                    pe.wait_ge(w_split, u + 1)
                    pe.wait_ge(g_lo_ready, i * 2 + (hb + 2))
                    for n_ in range(16):
                        f, hf = n_ // 2, n_ % 2
                        if not (isinstance(i, int) and i == 0 and l == 0 and n_ < 4):
                            pe.wait_ge(dn_out, i * 16 + (db + n_ - 3))
                        fs, hs_ = slice(f * P, (f + 1) * P), slice(hf * HALF, (hf + 1) * HALF)
                        product(ps[:, 4 + n_ % 4, :], [(ah[:, k, fs], al[:, k, fs], g_hi[:, k, hs_], g_lo[:, k, hs_]) for k in range(2)]
                                ).then_inc(dn_ps, 1)

                up(0, 0, b)
                up(1, 0, b + 1)
                up(0, 1, b + 2)
                down(0, b + 3)
                up(1, 1, b + 4)
                with pe.Fori(2, NI) as i:
                    up(0, i, i * 3 + (b - 1))
                    down(i - 1, i * 3 + b)
                    up(1, i, i * 3 + (b + 1))
                down(NI - 1, b + 3 * NI - 1)

            pe.wait_ge(mod_ready, 3)
            norm_sums(0)
            norm_spread(0)
            pe.wait_ge(n_lo, FT)
            ffn(0)
            pe.wait_ge(dn_out, 16 * NI)
            pe.wait_ge(conv1_in, 48)
            r1 = t_buf[0][:, :].rearrange("p (a n) -> p a n", n=P)
            pe.transpose(ps[:, 5, 0:4 * HT], r1[0:4 * HT, 0, :], ident[0:4 * HT, 0:4 * HT])
            pe.transpose(ps[:, 5, 4 * HT:8 * HT], r1[0:4 * HT, 1, :], ident[0:4 * HT, 0:4 * HT]).then_inc(rows_t, 1)
            norm_sums(1)
            pe.wait_ge(cst_ready, 2)
            norm_spread(1)
            pe.wait_ge(w_split, U_POOL + 1)
            ah, al = hl(SLOT[U_POOL])
            for n_ in range(2 * FT):
                f, hf = n_ // 2, n_ % 2
                g, o = f // 2, f % 2
                pe.wait_ge(n_lo, FT + 2 * g + 2)
                if n_ >= 4:
                    pe.wait_ge(pl_t, n_ - 3)
                cs, hs_ = slice(o * P, (o + 1) * P), slice(hf * HALF, (hf + 1) * HALF)
                product(ps[:, n_ % 4, :], [(ah[:, 2 * g + k, cs], al[:, 2 * g + k, cs], h_hi[:, 2 * g + k, hs_], h_lo[:, 2 * g + k, hs_]) for k in range(2)]
                        ).then_inc(pl_ps, 1)
            norm_sums(2)
            norm_spread(2)
            pe.wait_ge(n_lo, 3 * FT)
            ffn(1)
            norm_sums(3)
            pe.wait_ge(fin_scaled, FT)
            for t in range(TT):
                if t >= 2:
                    pe.wait_ge(fin_out, t - 1)
                for f in range(FT):
                    mm = pe.transpose(wide(2 * (t % 2))[:, f * P:(f + 1) * P], xT[:, f, t * P:(t + 1) * P], ident[:, :])
                mm.then_inc(fin_ps, 1)


_INS = ["x", "c", "ctx", "c_ctx", "ada_w", "ada_b", "norm_w", "attn_wqkv", "attn_q_gain", "attn_k_gain", "attn_wo",
        "pool_w", "pool_b", "pool_scale", "ffn_w_up", "ffn_conv_w", "ffn_conv_b", "ffn_w_down", "final_norm"]


def _tables(n_tokens, head_dim, grid_w=64, theta=10000.0, windows=(2, 4, 8, 16)):
    import numpy as np
    nf = head_dim // 4
    freqs = (np.float32(theta) ** (-np.arange(nf, dtype=np.float32) / np.float32(nf))).astype(np.float32)
    pos = np.arange(n_tokens)
    ang = [(v.astype(np.float32)[:, None] * freqs).astype(np.float32) for v in (pos // grid_w, pos % grid_w)]
    cos = np.concatenate([np.cos(a) for a in (ang[0], ang[0], ang[1], ang[1])], axis=1).astype(np.float32)
    sin = np.concatenate([-np.sin(ang[0]), np.sin(ang[0]), -np.sin(ang[1]), np.sin(ang[1])], axis=1).astype(np.float32)
    pad = windows[-1] // 2
    edge = np.ones((len(windows), 2, pad), np.float32)
    for g, w in enumerate(windows):
        for t in range(w // 2):
            edge[g, 0, t] = w / (t + w // 2)
            u = n_tokens - w // 2 + t
            edge[g, 1, t] = w / (min(u + w // 2 - 1, n_tokens - 1) - (u - w // 2) + 1)
    return cos, sin, edge.reshape(-1)


def kernel(**inputs):
    import numpy as _np
    import concourse.bacc as _bacc
    from concourse import mybir as _mybir
    from concourse.bass_utils import run_bass_kernel_spmd as _run

    nc = _bacc.Bacc("TRN2", target_bir_lowering=False, num_devices=1)
    arrays, args = {}, []
    cos, sin, edge = _tables(inputs["x"].shape[1], inputs["attn_q_gain"].shape[1])
    given = [(n, inputs[n]) for n in _INS] + [("rope_cos", cos), ("rope_sin", sin), ("pool_edge", edge)]
    for name, a in given:
        a = _np.ascontiguousarray(a)
        arrays[f"in_{name}_dram"] = a
        args.append(nc.dram_tensor(f"in_{name}_dram", a.shape, _mybir.dt.from_np(a.dtype), kind="ExternalInput").ap())
    args.append(nc.dram_tensor("out_0_dram", inputs["x"].shape, _mybir.dt.float32, kind="ExternalOutput").ap())
    hybrid_trunk(nc, *args)
    r = _run(nc, [arrays], core_ids=[0])
    return r.results[0]["out_0_dram"]
```

```python
import concourse.bass as bass
from concourse import mybir
from contextlib import ExitStack


def hybrid_trunk(nc, x, c, ctx, c_ctx, ada_w, ada_b, norm_w, wqkv, q_gain, k_gain, wo,
                 pool_w, pool_b, pool_scale, w_up, conv_w, conv_b, w_down, final_norm,
                 rope_cos, rope_sin, pool_edge, out):
    fp32 = mybir.dt.float32
    fp32r = mybir.dt.float32r
    ALU = mybir.AluOpType
    ACT = mybir.ActivationFunctionType
    AX = mybir.AxisListType

    P = 128
    NT, D = x.shape[1], x.shape[2]
    NC = ctx.shape[1]
    TT, CT, FT = NT // P, NC // P, D // P
    KT = TT + CT
    NK = KT * P
    HD = q_gain.shape[1]
    NH = wo.shape[1] // HD
    NKV = (wqkv.shape[2] // HD - NH) // 2
    GQ = NH // NKV
    HALF = 512
    FH = w_down.shape[1]
    HT = FH // P
    NI = HT // 2
    UC = 256
    MT = 6 * FT
    NU = 6 * D // UC
    EPS = 1e-6
    SCALE = float(HD) ** -0.5
    WINDOWS = (2, 4, 8, 16)
    PAD = WINDOWS[-1] // 2
    VW = 2 * HD + 2

    U_K, U_V, U_Q, U_WO = 0, 1, 2, 6
    NQU = NH * HD // UC
    NWO = D // UC
    U_F0 = U_WO + NWO
    U_POOL = U_F0 + 3 * NI
    U_F1 = U_POOL + 1

    KB = 1024
    base = (nc.sbuf_base + 63) // 64 * 64
    es = ExitStack()
    with es:
        def at(name, shape, off, dt=fp32):
            return nc.alloc_sbuf_tensor_at(name, shape, dt, offset=base + int(off))

        def sem(name):
            return es.enter_context(nc.semaphore(name))

        h_hi = at("h_hi", [P, FT, NT], 0, fp32r)
        h_lo = at("h_lo", [P, FT, NT], 32 * KB, fp32r)
        junk = at("junk", [P, D], 124 * KB)
        qa = [at(f"qa{i}", [P, NT], 4 * KB * i, fp32r) for i in range(2)]
        qb = [at(f"qb{i}", [P, NT], (8 + 4 * i) * KB, fp32r) for i in range(2)]
        ka = [at(f"ka{i}", [P, NK], (16 + 5 * i) * KB, fp32r) for i in range(2)]
        kb = [at(f"kb{i}", [P, NK], (26 + 5 * i) * KB, fp32r) for i in range(2)]
        p_hi = [at(f"p_hi{i}", [P, 2 * HALF], (36 + 4 * i) * KB, fp32r) for i in range(3)]
        p_lo = [at(f"p_lo{i}", [P, 2 * HALF], (48 + 4 * i) * KB, fp32r) for i in range(3)]
        o_t = [at(f"o_t{i}", [P, HALF], (60 + 2 * i) * KB) for i in range(2)]
        raw = [at("raw0", [P, FT * UC], 64 * KB), at("raw1", [P, FT * UC], 72 * KB),
               at("raw2", [P, FT * UC], 80 * KB)]
        ada_e = [at(f"ada_e{u}", [P, FT, UC], (4 + 8 * u) * KB) for u in range(7)]
        ada_raw = [at("ada_raw0", [P, FT, UC], 80 * KB), at("ada_raw1", [P, FT, UC], 88 * KB)]
        y_val = [at(f"y_val{j}", [P, NT], (88 + 4 * j) * KB) for j in range(2)]
        w_hi = [at(f"w_hi{i}", [P, FT * UC], (96 + 16 * i) * KB, fp32r) for i in range(3)]
        w_lo = [at(f"w_lo{i}", [P, FT * UC], (104 + 16 * i) * KB, fp32r) for i in range(3)]
        x_tok = at("x_tok", [P, TT, D], 128 * KB)
        q_tok = at("q_tok", [P, TT, D], 128 * KB)
        ch_hi = at("ch_hi", [P, FT, NC], 128 * KB, fp32r)
        ch_lo = at("ch_lo", [P, FT, NC], 136 * KB, fp32r)
        xT = at("xT", [P, FT, NT], 144 * KB)
        k_tok = at("k_tok", [P, KT, NKV * HD], 160 * KB)
        c_tok = at("c_tok", [P, CT, D], 160 * KB)
        v_hl = at("v_hl", [P, KT, NKV, VW], 170 * KB, fp32r)
        rows = at("rows", [P, 4, P], 170 * KB)
        cosT = at("cosT", [P, TT, HD], 172 * KB)
        sinT = at("sinT", [P, TT, HD], 174 * KB)
        gains = at("gains", [P, 2, HD], 176 * KB)
        x_re = [at("x_re0", [P, TT // 2, D], 80 * KB), at("x_re1", [P, TT // 2, D], 176 * KB)]
        t_buf = [at(f"t_buf{i}", [P, NT], (176 + 4 * i) * KB) for i in range(4)]
        y_gate = [at(f"y_gate{j}", [P, NT], (176 + 4 * j) * KB) for j in range(2)]
        g_hi = at("g_hi", [P, 2, NT], 184 * KB, fp32r)
        g_lo = at("g_lo", [P, 2, NT], 192 * KB, fp32r)
        g2_hi = at("g2_hi", [P, 2, NT], 112 * KB, fp32r)
        g2_lo = at("g2_lo", [P, 2, NT], 120 * KB, fp32r)
        PW = NT + 2 * PAD
        hp_d = [at(f"hp_d{i}", [P, PW], 184 * KB + i * 4 * PW) for i in range(2)]
        win_d = [at(f"win_d{i}", [P, PW], 184 * KB + (i + 2) * 4 * PW) for i in range(2)]
        hp_p = [at(f"hp_p{i}", [P, PW], 128 * KB + i * 4 * PW) for i in range(2)]
        win_p = [at("win_p0", [P, NT], 88 * KB), at("win_p1", [P, PW], 128 * KB + 8 * PW)]
        sq_a = [at(f"sq_a{i}", [P, NT], (128 + 4 * i) * KB) for i in range(4)]
        sq_b = [at("sq_b0", [P, NT], 92 * KB), at("sq_b1", [P, NT], 201 * KB)] + t_buf[2:4]
        sq_y = y_val + y_gate
        SQ = [sq_a, sq_y, sq_b, sq_y]
        S_BANK = [4, 0, 4, 0]
        o_sb = [at(f"o_sb{i}", [P, D], (4 * i) * KB) for i in range(4)]
        fn_bc = at("fn_bc", [P, D], 201 * KB)
        tabs = [at(f"tab{i}", [P, TT, HD], (191 + 2 * i) * KB) for i in range(4)]
        p32 = [at(f"p32_{i}", [P, 2 * HALF], (191 + 4 * i) * KB) for i in range(2)]
        acc = [at(f"acc{i}", [P, UC], (199 + i) * KB) for i in range(2)]
        id_r = at("id_r", [P, P], 199 * KB, fp32r)
        s1 = at("s1", [P, HALF], 201 * KB)
        s2 = at("s2", [P, HALF], 203 * KB)
        acc_x = [at(f"acc_x{i}", [P, UC], (112 + i) * KB) for i in range(4)]
        acc_c = [at(f"acc_c{i}", [P, UC], (116 + i) * KB) for i in range(4)]
        acc_w = acc + [at(f"acc_w{i}", [P, UC], (201 + i) * KB) for i in range(4)]
        acc_f = [at(f"acc_f{z}", [P, UC], (201 + z) * KB) for z in range(2)]
        t0 = [s1, s2]
        off = [205 * KB]

        def small(name, cols, dt=fp32):
            t = at(name, [P, cols], off[0], dt)
            off[0] += (4 * cols + 31) // 32 * 32
            return t

        NCONV = 4 * 2 * HT
        cst = small("cst", 2 * MT + 7 * FT + NCONV)
        C_NW, C_PB, C_PS, C_FN, C_CV = 2 * MT, 2 * MT + 4 * FT, 2 * MT + 5 * FT, 2 * MT + 6 * FT, 2 * MT + 7 * FT
        CV_W = [C_CV, C_CV + 2 * HT, C_CV + 4 * HT]
        CV_B = C_CV + 6 * HT
        ident = small("ident", P)
        one = small("one", 1)
        eps = small("eps", 1)
        mod = [small("mod0", MT), small("mod1", MT)]
        modc = small("modc", 2 * FT)
        nA = [small(f"nA{i}", FT) for i in range(5)]
        gs = small("gs", FT)
        gb = small("gb", FT)
        cvec = small("cvec", 2 * FT)
        csil = small("csil", 2 * FT)
        ss = small("ss", KT)
        std = small("std", KT)
        rstd = small("rstd", KT)
        mx = [at(f"mx{i}", [P, 3 * TT], 199.5 * KB + 96 * i) for i in range(2)]
        mxr = at("mxr", [P, TT], 199.5 * KB + 192)
        mneg = [at(f"mneg{i}", [P, TT], 199.5 * KB + 224 + 32 * i, fp32r) for i in range(2)]
        rden = at("rden", [P, 4], 199.5 * KB + 288)
        rows1 = at("rows1", [P, 2, P], 203 * KB)
        edge = at("edge", [P, 4 * 2 * PAD], 200.5 * KB)
        assert base + off[0] <= nc.sbuf_usable_end, (base + off[0], nc.sbuf_usable_end)

        ps = es.enter_context(nc.psum_tensor("ps", [P, 8, HALF], fp32))

        def wide(b, n=2):
            return ps[:, b:b + n, :].rearrange("p a b -> p (a b)")

        rows_in = sem("rows_in"); c_in = sem("c_in"); gain_in = sem("gain_in"); rope_in = sem("rope_in")
        x_in = [sem("x_in0"), sem("x_in1")]; ctx_in = sem("ctx_in"); conv1_in = sem("conv1_in")
        edge_in = sem("edge_in"); xre_in = [sem("xre_in0"), sem("xre_in1")]; out_done = [sem(f"out_done{i}") for i in range(4)]; fn_in = sem("fn_in")
        ada_in = [sem("ada_in0"), sem("ada_in1")]; adae_in = [sem(f"adae_in{u}") for u in range(8)]
        raw_in = [sem(f"raw_in{i}") for i in range(3)]
        hi_step = sem("hi_step")
        unit_here = sem("unit_here")
        w_split = sem("w_split")
        id_ready = sem("id_ready"); cst_init = sem("cst_init"); rows_t = sem("rows_t"); cst_ready = sem("cst_ready")
        csil_ready = sem("csil_ready"); vstep = sem("vstep"); astep = sem("astep")
        acc_dve = sem("acc_dve"); acc_pool = sem("acc_pool"); pstep = sem("pstep")
        ada_sum = sem("ada_sum"); adac_sum = sem("adac_sum"); adaf_sum = sem("adaf_sum"); adaf_out = sem("adaf_out"); mod_ready = sem("mod_ready")
        x_sq = sem("x_sq"); x_rstd = sem("x_rstd"); x_scaled = sem("x_scaled")
        xt_ready = sem("xt_ready"); t_ready = sem("t_ready"); h_split = sem("h_split")
        blk = sem("blk"); kq_out = sem("kq_out"); ssq_ready = sem("ssq_ready"); kq_std = sem("kq_std")
        roped = sem("roped"); v_hi_ready = sem("v_hi_ready"); v_out = sem("v_out"); tab_ready = sem("tab_ready")
        kT_ready = sem("kT_ready"); k_hi_ready = sem("k_hi_ready"); k_lo_ready = sem("k_lo_ready")
        qT_ready = sem("qT_ready"); q_hi_ready = sem("q_hi_ready"); q_lo_ready = sem("q_lo_ready")
        mx_ps = sem("mx_ps"); mx_red = sem("mx_red"); mneg_ready = sem("mneg_ready")
        mx0_ps = sem("mx0_ps"); mx0_red = sem("mx0_red"); ones_ready = sem("ones_ready")
        mrow_ps = sem("mrow_ps"); mrow_ready = sem("mrow_ready")
        s_ps = sem("s_ps"); p_ready = sem("p_ready"); phi_ready = sem("phi_ready"); plo_ready = sem("plo_ready"); plo2_ready = sem("plo2_ready")
        pv_step = sem("pv_step"); o_copied = sem("o_copied"); o_turned = sem("o_turned"); o_ready = sem("o_ready")
        oT_ps = sem("oT_ps"); oT_hi = sem("oT_hi"); oT_lo = sem("oT_lo")
        xr_ps = sem("xr_ps"); xr_out = sem("xr_out"); wo_ps = sem("wo_ps"); wo_out = sem("wo_out")
        sq_ready = sem("sq_ready"); sq_added = sem("sq_added"); sq_used = sem("sq_used"); ss_std = sem("ss_std"); ss_rstd = sem("ss_rstd")
        bc_ready = sem("bc_ready"); nt_ready = sem("nt_ready"); n_hi = sem("n_hi"); n_lo = sem("n_lo"); n_lo_p = sem("n_lo_p")
        up_ps = sem("up_ps"); y_ready = sem("y_ready"); cv_half = sem("cv_half"); cv_done = sem("cv_done")
        silu_ready = sem("silu_ready"); g_ready = sem("g_ready"); g_hi_ready = sem("g_hi_ready"); g_lo_ready = sem("g_lo_ready")
        dn_ps = sem("dn_ps"); dn_out = sem("dn_out")
        hp_ready = sem("hp_ready"); pooled = sem("pooled"); pooled_p = sem("pooled_p"); pmstep = sem("pmstep"); nl_step = sem("nl_step"); pmdstep = sem("pmdstep")
        pad_ready = sem("pad_ready"); pl_ps = sem("pl_ps"); pl_t = sem("pl_t"); pl_out = sem("pl_out")
        fin_ps = sem("fin_ps"); fin_out = sem("fin_out")

        NP_ = TT // 2
        BLKS = [(U_K, p) for p in range(NP_ + 1)] + [(U_V, p) for p in range(NP_ + 1)] \
            + [(U_Q + u, p) for u in range(NQU) for p in range(NP_)]
        KQ = [b for b, (u, _) in enumerate(BLKS) if u != U_V]
        VB = [b for b, (u, _) in enumerate(BLKS) if u == U_V]
        EARLY = 2 * D // UC
        NQA = D // UC * 2
        U_WA = EARLY + NQA
        U_FA = 2 * NU - 2 * (NI - 1)
        NWA = U_FA - U_WA
        NA1 = U_FA - NU
        ADA_AT = {6 + 13 * i // 7: EARLY + i for i in range(NQA)}
        NG = NWO * 4
        POOL_ADA = range(EARLY, U_WA + 4, 2)
        DVE_ADA = [u for u in range(EARLY, U_FA) if u not in POOL_ADA]

        NE = EARLY // 2
        U_BOTH = EARLY - 3
        BEFORE = {acc_dve: NE + 1, acc_pool: NE - 1}
        ada_e = ada_e + [ada_raw[1]]

        WO_ADA = {g: [u] for g, u in zip((0, 2, 3, 4, 5, 6, 7, 8, 9, 10), [u for u in DVE_ADA if u >= U_WA])}

        def acc_of(u):
            sem_, units = (acc_pool, POOL_ADA) if u in POOL_ADA else (acc_dve, DVE_ADA)
            return sem_, BEFORE[sem_] + len([v for v in units if v <= u])

        def acc_at(u):
            if u < U_WA:
                return acc[u % 2], (u - 2 if u >= EARLY + 2 else None)
            k = u - U_WA
            return acc_w[k % 6], (u - 6 if k >= 6 else None)

        SLOT = [u % 2 for u in range(U_F0)] + ([0, 1] + [0, 2, 1] * (NI - 1) + [0]) + [1] + ([0, 1] + [0, 2, 1] * (NI - 1) + [0])
        NUNITS = len(SLOT)

        def nth(u):
            same = [v for v in range(u + 1) if SLOT[v] == SLOT[u]]
            return len(same), (same[-2] if len(same) > 1 else None)

        def cols_of(w, c0):
            return w[:, c0:c0 + UC].rearrange("(t p) n -> p t n", p=P)

        def unit_src(u):
            if u == U_K:
                return cols_of(wqkv[0], NH * HD)
            if u == U_V:
                return cols_of(wqkv[0], (NH + NKV) * HD)
            if u < U_WO:
                return cols_of(wqkv[0], (u - U_Q) * UC)
            if u < U_F0:
                return cols_of(wo[0], (u - U_WO) * UC)
            if u == U_POOL:
                return pool_w[0].rearrange("g (t p) e -> p (g t) e", p=P)

        def used(u):
            if u < U_WO:
                return blk, max(b for b, (v, _) in enumerate(BLKS) if v == u) + 1
            if u < U_F0:
                return wo_ps, 4 * (u - U_WO + 1)
            if u == U_POOL:
                return pl_ps, 2 * FT
            l, v = (0, u - U_F0) if u < U_POOL else (1, u - U_F1)
            if v >= 3 * NI - 2:
                return dn_ps, 2 * FT * NI * (l + 1)
            i, kind = (0, 2 * v) if v < 2 else ((v + 1) // 3, (v + 1) % 3)
            assert kind != 1
            return up_ps, 4 * NI * l + 4 * i + kind + 2

        TURN_AT = {0: range(FT + 3, 2 * FT), 1: range(2 * FT, 2 * FT + 3), 2: range(2 * FT + 3, 3 * FT)}
        MOD_AT = max(ADA_AT) + 4
        CTX_AT = FT + 3
        MODC_AT = 2 * FT
        SPLIT_AT = {EARLY: 2, EARLY + 2: 3, EARLY + 4: 4, EARLY + 6: 5}
        SPLIT_WO = {U_WA + 2: U_WO + 2}
        NPA = NE - 1 + len(POOL_ADA)
        R2 = [0, 3 * (NI - 1)]

        def raw3(s):
            return raw[s][:, :].rearrange("p (t n) -> p t n", n=UC)

        def hl(s):
            return (w_hi[s][:, :].rearrange("p (t n) -> p t n", n=UC),
                    w_lo[s][:, :].rearrange("p (t n) -> p t n", n=UC))

        def hl_down(s):
            return (w_hi[s][:, :].rearrange("p (t n) -> p t n", n=D),
                    w_lo[s][:, :].rearrange("p (t n) -> p t n", n=D))

        def heads(t):
            return t.rearrange("p a (h d) -> p a h d", d=HD)

        NS = KT
        HS = NS // 2
        NM = 3 * TT
        ROW = TURN_K = NS - 3
        TURN_Q = NS - 2
        LC = 608

        def pieces(s):
            h, e = divmod(s, NS)
            g, k = (h + 1, e + 1) if e < ROW else (h + 2, 0)
            return g, ([3 * k + i for i in range(3)] if g < NH and (e < ROW or e == NS - 1) else [])

        def new_k(s):
            h, e = divmod(s, NS)
            return (h + 2) // GQ if e == TURN_K and h + 2 < NH and (h + 2) % GQ == 0 else None

        HF = FT // 2
        MIX_IN = [f for i in range(HF) for f in (i, HF + i)]
        MIX_OUT = [f for i in range(0, HF, 2) for f in (i, i + 1, HF + i, HF + i + 1)]

        def is_step(i, k):
            return isinstance(i, int) and i == k

        FB = [U_F0, U_F1]

        def new_q(s):
            h, e = divmod(s, NS)
            if e == TURN_Q and h + 2 < NH:
                return h + 2, (h + 2) % GQ != 0
            return None, False

        block = es.enter_context(nc.Block())

        def mix_tiles(e, win, hp, f0, step, done, lo_done, between=()):
            n = [0]

            def link(ins):
                n[0] += 1
                ins.then_inc(step, 1)
                e.wait_ge(step, n[0])

            def lo(i):
                e.wait_ge(n_hi, FT + 2 * i + (1 if f0 == 0 else 2))
                e.tensor_tensor(h_lo[:, f0 + i, :], hp[i % 2][:, PAD:PAD + NT],
                                h_hi[:, f0 + i, :].bitcast(fp32), ALU.subtract).then_inc(lo_done, 1)

            e.wait_ge(dn_out, 2 * FT * NI)
            for t in hp:
                e.memset(t[:, 0:PAD], 0.0).then_inc(pad_ready, 1)
                e.memset(t[:, PAD + NT:PW], 0.0).then_inc(pad_ready, 1)
            for i in range(HF):
                for work in (between[i] if between else ()):
                    work()
                h = hp[i % 2]
                g = (f0 + i) * len(WINDOWS) // FT
                W = WINDOWS[g]
                o0 = PAD if win is win_d else 0
                at0 = [o0, PAD]
                e.wait_ge(hp_ready, 2 * i + (1 if f0 == 0 else 2))
                if i == 0:
                    e.wait_ge(pad_ready, 8)
                else:
                    e.wait_ge(done, i)
                m = W // 2 - 1
                for lev in range(g + 1):
                    r = 2 ** max(lev - 1, 0)
                    if lev > 0:
                        m -= r
                    d = (g - lev) % 2
                    lo_, hi_ = (m + 1, m) if lev == 0 else (m + r, m - r)
                    s_, so = (h, PAD) if lev == 0 else (win[1 - d], at0[1 - d])
                    link(e.tensor_tensor(win[d][:, at0[d] - m:at0[d] + NT + m], s_[:, so - lo_:so - lo_ + NT + 2 * m],
                                         s_[:, so - hi_:so - hi_ + NT + 2 * m], ALU.add))
                    if lev == 0 and i >= 1:
                        lo(i - 1)
                w0 = win[0]
                E0 = edge[:, 2 * g * PAD:2 * g * PAD + W // 2]
                E1 = edge[:, (2 * g + 1) * PAD:(2 * g + 1) * PAD + W // 2]
                if i == 0:
                    e.wait_ge(edge_in, 16)
                e.tensor_tensor(w0[:, o0:o0 + W // 2], w0[:, o0:o0 + W // 2], E0, ALU.mult).then_inc(step, 1)
                n[0] += 1
                link(e.tensor_tensor(w0[:, o0 + NT - W // 2:o0 + NT], w0[:, o0 + NT - W // 2:o0 + NT], E1, ALU.mult))
                if win is win_p:
                    link(e.tensor_scalar(w0[:, o0:o0 + NT], w0[:, o0:o0 + NT], 1.0 / W, 1.0, ALU.mult, ALU.mult))
                    e.tensor_tensor(h[:, PAD:PAD + NT], w0[:, o0:o0 + NT], h[:, PAD:PAD + NT], ALU.subtract).then_inc(done, 1)
                else:
                    e.scalar_tensor_tensor(out=h[:, PAD:PAD + NT], in0=w0[:, o0:o0 + NT], scalar=1.0 / W,
                                           in1=h[:, PAD:PAD + NT], op0=ALU.mult, op1=ALU.subtract).then_inc(done, 1)
            lo(HF - 1)

        @block.sync
        def _(sp):
            def ada(u):
                l, v = divmod(u, NU)
                if u < EARLY:
                    sp.dma_start(ada_e[u][:, :, :], ada_w[l][:, v * UC:(v + 1) * UC].rearrange("(p t) n -> p t n", t=FT)
                                 ).then_inc(adae_in[u], 16)
                    return
                if u == EARLY + 1:
                    sp.wait_ge(acc_dve, NE + 1)
                    sp.wait_ge(acc_pool, NE - 1)
                if u >= EARLY + 2:
                    sp.wait_ge(*acc_of(u - 2))
                sp.dma_start(ada_raw[u % 2][:, :, :],
                             ada_w[l][:, v * UC:(v + 1) * UC].rearrange("(p t) n -> p t n", t=FT)
                             ).then_inc(ada_in[u % 2], 16)

            def load(u):
                n_, prev = nth(u)
                if prev is not None:
                    sp.wait_ge(w_split, prev + 1)
                sp.dma_start(raw3(SLOT[u]), unit_src(u)).then_inc(raw_in[SLOT[u]], 16)

            for u in range(EARLY):
                ada(u)
                if u == 1:
                    sp.wait_ge(rows_in, 16 * 8)
                if u == 4:
                    load(0)
            load(1); load(2); load(3)
            for u in range(EARLY, U_WA):
                ada(u)
                if u == EARLY + 1:
                    load(4)
                if u == EARLY + 3:
                    load(5)
                if u == EARLY + 5:
                    load(6)
            load(7); load(8); load(9)
            sp.wait_ge(*acc_of(U_WA - 2))
            sp.wait_ge(*acc_of(U_WA - 1))
            sp.dma_start(x_re[0][:, :, :], x[0, 0:NT // 2, :].rearrange("(t p) n -> p t n", p=P)).then_inc(xre_in[0], 16)
            sp.wait_ge(pv_step, NH * NS)
            sp.dma_start(x_re[1][:, :, :], x[0, NT // 2:NT, :].rearrange("(t p) n -> p t n", p=P)).then_inc(xre_in[1], 16)

            def load_up(l, s, col, n_wait):
                if n_wait is not None:
                    sp.wait_ge(w_split, n_wait)
                sp.dma_start(raw3(s), w_up[l][:, bass.ds(col, UC)].rearrange("(t p) n -> p t n", p=P)
                             ).then_inc(raw_in[s], 16)

            def load_down(l, row, n_wait, n_ada=None):
                sp.wait_ge(w_split, n_wait)
                if n_ada is not None:
                    sp.wait_ge(acc_pool, n_ada)
                sp.dma_start(raw[2][:, :].rearrange("p (t n) -> p t n", n=D),
                             w_down[l][bass.ds(row, 2 * P), :].rearrange("(t p) n -> p t n", p=P)
                             ).then_inc(raw_in[2], 16)

            def load_ada(z, col):
                sp.dma_start(raw3(2), ada_w[1][:, bass.ds(col, UC)].rearrange("(p t) n -> p t n", t=FT)
                             ).then_inc(raw_in[2], 16)

            sp.wait_ge(xr_ps, FT)
            for u in range(U_WA, U_FA):
                ada(u)
                if u == U_WA + 7:
                    load_up(0, 0, 0, nth(U_F0)[1] + 1)
            load_up(0, 1, FH, nth(U_F0 + 1)[1] + 1)
            sp.wait_ge(acc_dve, NE + 1 + len(DVE_ADA))
            sp.wait_ge(acc_pool, NPA)
            for l in range(2):
                b = FB[l]
                if l == 1:
                    sp.wait_ge(w_split, nth(U_POOL)[1] + 1)
                    sp.dma_start(raw3(1), unit_src(U_POOL)).then_inc(raw_in[1], 16)
                    load_up(1, 0, 0, nth(U_F1)[1] + 1)
                    load_up(1, 1, FH, nth(U_F1 + 1)[1] + 1)
                def load_ada_pair(i):
                    sp.wait_ge(w_split, i * 3 + (b + 1))
                    load_ada(0, i * (2 * UC) + (NA1 - 2) * UC)
                    sp.wait_ge(acc_pool, i * 2 + (NPA - 1))
                    load_ada(1, i * (2 * UC) + (NA1 - 1) * UC)

                with sp.Fori(1, NI - 1) as i:
                    load_up(l, 0, i * UC, i * 3 + (b - 2))
                    load_down(l, (i - 1) * UC, i * 3 + (b - 2), i * 2 + (NPA - 2) if l == 0 else None)
                    if l == 0:
                        load_ada_pair(i)
                    load_up(l, 1, i * UC + FH, i * 3 + (b - 1))
                i = NI - 1
                load_up(l, 0, i * UC, i * 3 + (b - 2))
                load_down(l, (i - 1) * UC, i * 3 + (b - 2), i * 2 + (NPA - 2) if l == 0 else None)
                load_up(l, 1, i * UC + FH, i * 3 + (b - 1))
                sp.wait_ge(w_split, 3 * (NI - 1) + b)
                sp.dma_start(raw[0][:, :].rearrange("p (t n) -> p t n", n=D),
                             w_down[l][(NI - 1) * UC:NI * UC, :].rearrange("(t p) n -> p t n", p=P)
                             ).then_inc(raw_in[0], 16)
                if l == 0:
                    load_ada_pair(i)
                    sp.wait_ge(acc_pool, NPA + 2 * (NI - 1))
            for t in range(TT):
                sp.wait_ge(fin_out, t + 1)
                sp.dma_start(out[0, t * P:(t + 1) * P, :], o_sb[t % 4][:, :]).then_inc(out_done[t % 4], 16)
            for o in out_done:
                sp.wait_ge(o, 16 * TT // 4)

        @block.gpsimd
        def _(pool):
            chain = [0]
            PER_UNIT = FT + 2

            def split(dst_hi, dst_lo, src, done, k):
                pool.tensor_scalar(dst_hi, src, 1.0, 1.0, ALU.mult, ALU.mult).then_inc(hi_step, 1)
                pool.wait_ge(hi_step, k + 1)
                pool.tensor_tensor(dst_lo, src, dst_hi.bitcast(fp32), ALU.subtract).then_inc(done, 1)

            def split_unit(s, n_raw, last, k):
                pool.wait_ge(raw_in[s], n_raw)
                if last is not None:
                    pool.wait_ge(*last)
                pool.sem_inc(unit_here, 1)
                split(w_hi[s][:, :], w_lo[s][:, :], raw[s][:, :], w_split, k)

            pool.memset(ident[:, :], 0.0).then_inc(id_ready, 1)
            pool.wait_ge(id_ready, 1)
            pool.affine_select(out=ident[:, :], in_=ident[:, :], compare_op=ALU.not_equal, fill=1.0,
                               base=0, pattern=[[-1, P]], channel_multiplier=1).then_inc(id_ready, 1)

            def weigh(w, c0, dst, link, inc):
                for t in range(FT):
                    inc(pool.tensor_scalar(w[:, t, :], w[:, t, :], csil[:, c0 + t:c0 + t + 1], 1.0, ALU.mult, ALU.mult), t)
                n = FT // 2
                while n > 1:
                    link(pool.tensor_tensor(w[:, 0:n, :], w[:, 0:n, :], w[:, n:2 * n, :], ALU.add))
                    n //= 2
                return pool.tensor_tensor(dst[:, :], w[:, 0, :], w[:, 1, :], ALU.add)

            def ada(u):
                if u == 1:
                    pool.wait_ge(csil_ready, 1)
                if u >= EARLY:
                    pool.wait_ge(ada_in[u % 2], 16 * ((u - EARLY) // 2 + 1))
                    if acc_at(u)[1] is not None:
                        pool.wait_ge(ada_sum, acc_at(u)[1] + 1)
                else:
                    pool.wait_ge(adae_in[u], 16)
                    pool.wait_ge(acc_dve, u // 2 + 1 + (u > U_BOTH))

                def inc(ins, t):
                    chain[0] += 1
                    ins.then_inc(pstep, 1)
                    if t == FT - 1:
                        pool.wait_ge(pstep, chain[0])

                weigh(ada_e[u] if u < EARLY else ada_raw[u % 2], FT if u < EARLY else 0,
                      acc_c[u // 2] if u < EARLY else acc_at(u)[0], lambda ins: inc(ins, FT - 1), inc).then_inc(acc_pool, 1)

            def split_next(u):
                n_, prev = nth(u)
                if u == 1:
                    pool.wait_ge(mod_ready, 2)
                split_unit(SLOT[u], 16 * n_, None if prev is None else used(prev), u)

            ada(1)
            split_next(0)
            for u in [v for v in range(3, EARLY, 2) if v != U_BOTH]:
                ada(u)
            split_next(1)
            for u in range(EARLY, U_WA, 2):
                ada(u)
                if u in SPLIT_AT:
                    split_next(SPLIT_AT[u])
            for u in range(2 + len(SPLIT_AT), U_WO + 2):
                split_next(u)
            pool.wait_ge(blk, len(BLKS))
            pool.wait_ge(w_split, U_WO + 2)
            for i in range(2):
                pool.memset(kb[i][HD:HD + 1, :].bitcast(fp32), 1.0).then_inc(ones_ready, 1)
                pool.wait_ge(ones_ready, i + 1)
            for s in range(NH * NS):
                pool.wait_ge(p_ready, s + 1)
                if s >= 3:
                    pool.wait_ge(pv_step, s - 2)
                pool.tensor_scalar(p_hi[s % 3][:, :], p32[s % 2][:, :], 1.0, 1.0, ALU.mult, ALU.mult
                                   ).then_inc(phi_ready, 1)
                pool.wait_ge(phi_ready, s + 1)
                pool.tensor_tensor(p_lo[s % 3][:, LC:], p32[s % 2][:, LC:], p_hi[s % 3][:, LC:].bitcast(fp32),
                                   ALU.subtract).then_inc(plo2_ready, 1)
            for u in [v for v in POOL_ADA if v >= U_WA]:
                ada(u)
                if u in SPLIT_WO:
                    split_next(SPLIT_WO[u])
            split_next(U_WO + 3); split_next(U_F0); split_next(U_F0 + 1)

            def ada_ffn(i, z):
                pool.wait_ge(raw_in[2], i * 48 + (16 * z - 16))
                if z == 0:
                    pool.wait_ge(adaf_out, i)
                pool.sem_inc(unit_here, 1)
                base_ = chain[0]
                m = [0]

                def inc(ins, t):
                    m[0] += 1
                    ins.then_inc(pstep, 1)
                    if t == FT - 1:
                        pool.wait_ge(pstep, i * (2 * PER_UNIT) + ((z - 2) * PER_UNIT + m[0] + base_))

                weigh(raw3(2), 0, acc_f[z], lambda ins: inc(ins, FT - 1), inc).then_inc(acc_pool, 1)
                assert m[0] == PER_UNIT

            def norm_lo(k):
                S_ = mod[k // 2]
                for f in range(1, FT, 2):
                    pool.wait_ge(n_hi, k * FT + f + 1)
                    pool.tensor_scalar(t_buf[f % 4][:, :], t_buf[f % 4][:, :], S_[:, 3 * FT + f:3 * FT + f + 1], 1.0,
                                       ALU.add, ALU.mult).then_inc(nl_step, 1)
                    pool.wait_ge(nl_step, k // 2 * HF + f // 2 + 1)
                    pool.tensor_tensor(h_lo[:, f, :], t_buf[f % 4][:, :], h_hi[:, f, :].bitcast(fp32), ALU.subtract
                                       ).then_inc(n_lo_p, 1)

            for l in range(2):
                b = FB[l]
                if l == 1:
                    split_next(U_POOL)
                    mix_tiles(pool, win_p, hp_p, 0, pmstep, pooled_p, n_lo_p)
                    split_next(U_F1)
                    split_next(U_F1 + 1)
                norm_lo(2 * l)
                nv, ng = nth(b)[0], nth(b + 1)[0]
                nr = 3 if l == 0 else 1
                ub = 4 * NI * l
                def splits(i):
                    split_unit(0, i * 16 + 16 * nv, (up_ps, i * 4 + (ub - 2)), i * 3 + (b - 1))
                    split_unit(2, i * (16 * nr) + 16 * (R2[l] + 1 - nr), (up_ps, i * 4 + (ub - 1)), i * 3 + b)
                    if l == 0 and not is_step(i, NI - 1):
                        ada_ffn(i, 0); ada_ffn(i, 1)
                    split_unit(1, i * 16 + 16 * ng, (up_ps, i * 4 + ub), i * 3 + (b + 1))
                with pool.Fori(1, NI - 1) as i:
                    splits(i)
                splits(NI - 1)
                if l == 0:
                    ada_ffn(NI - 1, 0); ada_ffn(NI - 1, 1)
                split_unit(0, 16 * (nv + NI), (up_ps, NI * 4 + ub - 2), NI * 3 + b - 1)

        @block.scalar
        def _(act):
            act.dma_start(cvec[:, 0:FT], c[0].rearrange("(p t) -> p t", t=FT)).then_inc(c_in, 16)
            act.dma_start(cvec[:, FT:2 * FT], c_ctx.rearrange("(p t) -> p t", t=FT)).then_inc(c_in, 16)
            act.dma_start(rows[0:2 * MT, 0, :], ada_b.rearrange("l (j p) -> (l j) p", p=P)).then_inc(rows_in, 16)
            act.dma_start(rows[0:4 * FT, 1, :], norm_w.rearrange("l k (j p) -> (l k j) p", p=P)).then_inc(rows_in, 16)
            for n_, v in enumerate((pool_b[0], pool_scale[0], final_norm)):
                act.dma_start(rows[(4 + n_) * FT:(5 + n_) * FT, 1, :], v.rearrange("(j p) -> j p", p=P)).then_inc(rows_in, 16)
            cw0 = conv_w[0].rearrange("k (j p) -> (k j) p", p=P)
            cb0 = conv_b[0].rearrange("(j p) -> j p", p=P)
            act.dma_start(rows[0:4 * HT, 2, :], cw0[0:4 * HT, :]).then_inc(rows_in, 16)
            act.dma_start(rows[0:2 * HT, 3, :], cw0[4 * HT:6 * HT, :]).then_inc(rows_in, 16)
            act.dma_start(rows[2 * HT:4 * HT, 3, :], cb0).then_inc(rows_in, 16)
            for hf in range(2):
                act.dma_start(x_tok[:, hf * TT // 2:(hf + 1) * TT // 2, :],
                              x[0, hf * NT // 2:(hf + 1) * NT // 2, :].rearrange("(t p) n -> p t n", p=P)
                              ).then_inc(x_in[hf], 16)
            act.dma_start(gains[:, 0, :], q_gain.to_broadcast((P, HD))).then_inc(gain_in, 16)
            act.dma_start(gains[:, 1, :], k_gain.to_broadcast((P, HD))).then_inc(gain_in, 16)
            act.dma_start(cosT[:, :, :], rope_cos.rearrange("(t p) d -> p t d", p=P)).then_inc(rope_in, 16)
            act.dma_start(sinT[:, :, :], rope_sin.rearrange("(t p) d -> p t d", p=P)).then_inc(rope_in, 16)
            act.wait_ge(c_in, 32)
            act.activation(csil[:, :], cvec[:, :], ACT.Silu).then_inc(csil_ready, 1)

            def tok(t):
                return x_tok[:, t, :] if t < TT else c_tok[:, t - TT, :]

            def norm_rows(t0_, t1, k):
                for t in range(t0_, t1):
                    if t % (TT // 2) == 0:
                        act.wait_ge(x_in[t * 2 // TT] if t < TT else ctx_in, 16)
                    if t >= 1:
                        act.wait_ge(x_sq, t + k)
                    act.activation(junk[:, :], tok(t), ACT.Square, accum_out=ss[:, t:t + 1]).then_inc(x_sq, 1)
                act.wait_ge(x_sq, t1 + k)
                act.activation(std[:, t0_:t1], ss[:, t0_:t1], ACT.Sqrt, bias=eps[:, :], scale=1.0 / D).then_inc(x_sq, 1)
                act.wait_ge(x_rstd, k + 1)
                for t in range(t0_, t1):
                    act.activation(tok(t), tok(t), ACT.Copy, scale=rstd[:, t:t + 1]).then_inc(x_scaled, 1)

            act.wait_ge(cst_init, 2)
            norm_rows(0, TT, 0)
            act.dma_start(c_tok[:, :, :], ctx[0].rearrange("(t p) n -> p t n", p=P)).then_inc(ctx_in, 16)
            for n_ in range(3 * FT):
                f, part = n_ % FT, n_ // FT
                w = HALF if part < 2 else NC
                if n_ == CTX_AT:
                    norm_rows(TT, KT, 1)
                if n_ % (2 * FT) == 0:
                    act.wait_ge(mod_ready, part // 2 + 1)
                act.wait_ge(xt_ready, n_ + 1)
                if n_ >= 2:
                    act.wait_ge(h_split, n_ - 1)
                A_, S_ = (nA[0], mod[0]) if part < 2 else (nA[1], modc)
                act.activation(t0[n_ % 2][:, 0:w], ps[:, 4 + n_ % 3, 0:w], ACT.Identity,
                               bias=S_[:, f:f + 1], scale=A_[:, f:f + 1]).then_inc(t_ready, 1)

            def k_copy(j):
                act.wait_ge(kT_ready, j + 1)
                if j >= 2:
                    act.wait_ge(s_ps, 2 * NS * (j - 1) * GQ)
                act.activation(ka[j % 2][0:HD, :], wide(5, 3)[0:HD, 0:NK], ACT.Copy).then_inc(k_hi_ready, 1)
                act.wait_ge(k_hi_ready, 2 * j + 1)
                act.activation(kb[j % 2][0:HD, :], ka[j % 2][0:HD, :].bitcast(fp32), ACT.Copy).then_inc(k_hi_ready, 1)

            kq, vb = 0, 0
            for b, (u, p) in enumerate(BLKS):
                act.wait_ge(blk, b + 1)
                if b == len(BLKS) - 1:
                    k_copy(0)
                src = ps[:, b % 4, :].rearrange("p (a n) -> p a n", a=2)
                if u == U_V:
                    if vb == 0:
                        act.wait_ge(roped, kq)
                    act.activation(v_hl[:, 2 * p:2 * p + 2, :, 0:HD], heads(src), ACT.Copy).then_inc(v_hi_ready, 1)
                    vb += 1
                    continue
                dst = k_tok[:, 2 * p:2 * p + 2, :] if u == U_K else q_tok[:, 2 * p:2 * p + 2, (u - U_Q) * UC:(u - U_Q + 1) * UC]
                act.activation(dst, src, ACT.Copy).then_inc(astep, 1)
                if kq >= 1:
                    act.wait_ge(roped, kq)
                else:
                    act.wait_ge(h_split, 3 * FT)
                act.activation(s1[:, :], ps[:, b % 4, :], ACT.Square).then_inc(kq_out, 1)
                act.wait_ge(ssq_ready, kq + 1)
                act.activation(std[:, 0:8], ss[:, 0:8], ACT.Sqrt, bias=eps[:, :], scale=1.0 / HD).then_inc(kq_std, 1)
                kq += 1

            def q_copy(h):
                act.wait_ge(qT_ready, h + 1)
                if h >= 2:
                    act.wait_ge(s_ps, 2 * NS * (h - 1))
                act.activation(qa[h % 2][0:HD, :], wide(6)[0:HD, :], ACT.Copy).then_inc(q_hi_ready, 1)
                act.wait_ge(q_hi_ready, 2 * h + 1)
                act.activation(qa[h % 2][HD:2 * HD, :], qa[h % 2][0:HD, :].bitcast(fp32), ACT.Copy).then_inc(q_hi_ready, 1)

            def mrow(h):
                act.wait_ge(mrow_ps, h + 1)
                act.activation(qb[h % 2][HD:HD + 1, :], wide(6)[0:1, :], ACT.Copy).then_inc(mrow_ready, 1)

            def exps(s):
                act.wait_ge(s_ps, 2 * s + 2)
                if s >= 2:
                    act.wait_ge(plo_ready, s - 1)
                    act.wait_ge(plo2_ready, s - 1)
                b = 2 * (s % 2)
                act.activation(p32[s % 2][:, :], wide(b), ACT.Exp, scale=SCALE).then_inc(p_ready, 1)

            def o_copy(n_):
                act.wait_ge(pv_step, (n_ + 1) * (KT // 2))
                if n_ >= 2:
                    act.wait_ge(o_turned, n_ - 1)
                act.activation(o_t[n_ % 2][0:HD + 1, :], ps[0:HD + 1, 4, :], ACT.Copy).then_inc(o_copied, 1)

            q_copy(0)
            act.activation(std[:, 8:9], eps[:, :], ACT.Exp)
            mrow(0)
            act.wait_ge(roped, len(KQ))
            exps(0); exps(1)
            q_copy(1)
            for s in range(NH * NS):
                h, e = divmod(s, NS)
                if s % HS == 0 and s > 0:
                    o_copy(s // HS - 1)
                if s > 0 and new_k(s - 1) is not None:
                    k_copy(new_k(s - 1))
                if s > 0 and new_q(s - 1)[0] is not None and not new_q(s - 1)[1]:
                    q_copy(h + 2)
                if new_q(s)[1]:
                    q_copy(h + 2)
                if s + 2 < NH * NS:
                    exps(s + 2)
                if e == ROW and h + 1 < NH:
                    mrow(h + 1)
            o_copy(2 * NH - 1)

            for n_ in range(2 * FT):
                f, hf = n_ // 2, n_ % 2
                act.wait_ge(oT_ps, n_ + 1)
                act.activation(h_hi[:, f, hf * HALF:(hf + 1) * HALF], ps[:, n_ % 4, :], ACT.Copy).then_inc(oT_hi, 1)
            for n_ in range(2 * FT):
                f, hf = n_ % FT, n_ // FT
                act.wait_ge(xr_ps, n_ + 1)
                act.activation(xT[:, f, hf * HALF:(hf + 1) * HALF], ps[:, 4 + n_ % 2, :], ACT.Copy).then_inc(xr_out, 1)

            def square(k, m):
                R = len(SQ[k]) - 1
                if m > R:
                    act.wait_ge(sq_added, k * (FT - 1) + m - R)
                f = MIX_OUT[m] if k == 2 else m
                act.activation(SQ[k][(m - 1) % R + 1 if m else 0][:, :], xT[:, f, :], ACT.Square).then_inc(sq_ready, 1)

            def norm_std(k):
                act.wait_ge(sq_used, k + 1)
                act.activation(std[:, 0:TT], ps[:, S_BANK[k], 0:TT], ACT.Sqrt, bias=eps[:, :], scale=1.0 / D).then_inc(ss_std, 1)

            def norm_hi(k, S_, c0):
                for f in range(FT):
                    act.wait_ge(nt_ready, k * FT + f + 1)
                    act.activation(h_hi[:, f, :], t_buf[f % 4][:, :], ACT.Identity,
                                   bias=S_[:, c0 + f:c0 + f + 1]).then_inc(n_hi, 1)

            def ffn(l):
                ub, hb, db = 4 * NI * l, 2 * NI * l, 16 * NI * l

                def y(j, gate, i):
                    n_ = i * 4 + (ub + 2 * gate + j)
                    act.wait_ge(up_ps, n_ + 1)
                    if not (is_step(i, 0) and l == 0):
                        act.wait_ge(g_lo_ready if gate else g_ready, i * 2 + (hb + j - 1))
                    t = (y_gate if gate else y_val)[j]
                    q = HT * gate + j
                    act.activation(t[:, :], wide(2 * j), ACT.Identity,
                                   bias=cst[:, bass.ds(i * 2 + (CV_B + q), 1)],
                                   scale=cst[:, bass.ds(i * 2 + (CV_W[1] + q), 1)]).then_inc(y_ready, 1)

                def step(i, hi=g_hi):
                    for j in range(2):
                        y(j, 0, i)
                    for j in range(2):
                        y(j, 1, i)
                    for j in range(2):
                        act.wait_ge(cv_done, i * 4 + (ub + 2 + j + 1))
                        act.activation(y_gate[j][:, :], y_gate[j][:, :], ACT.Silu).then_inc(silu_ready, 1)
                    for j in range(2):
                        act.wait_ge(g_ready, i * 2 + (hb + j + 1))
                        if not (is_step(i, NI - 1) or is_step(i, 0) and l == 0):
                            act.wait_ge(dn_ps, i * 16 + db)
                        act.activation(hi[:, j, :], y_gate[j][:, :], ACT.Copy).then_inc(g_hi_ready, 1)

                step(0)
                with act.Fori(1, NI - 1) as i:
                    step(i)
                step(NI - 1, g2_hi)

            for f in range(FT):
                act.wait_ge(wo_out, 2 * f + 2)
                square(0, f)
            norm_std(0)
            act.wait_ge(mod_ready, 4)
            norm_hi(0, mod[0], 3 * FT)
            cw1 = conv_w[1].rearrange("k (j p) -> (k j) p", p=P)
            cb1 = conv_b[1].rearrange("(j p) -> j p", p=P)
            act.dma_start(rows1[0:4 * HT, 0, :], cw1[0:4 * HT, :]).then_inc(conv1_in, 16)
            act.dma_start(rows1[0:2 * HT, 1, :], cw1[4 * HT:6 * HT, :]).then_inc(conv1_in, 16)
            act.dma_start(rows1[2 * HT:4 * HT, 1, :], cb1).then_inc(conv1_in, 16)
            act.dma_start(edge[:, :], pool_edge.rearrange("(a n) -> a n", a=1).to_broadcast((P, 4 * 2 * PAD))).then_inc(edge_in, 16)
            act.wait_ge(n_lo, HF)
            act.wait_ge(n_lo_p, HF)
            ffn(0)
            for f in range(FT):
                act.wait_ge(dn_out, 16 * (NI - 1) + 2 * f + 2)
                square(1, f)
            norm_std(1)
            act.wait_ge(mod_ready, 5)

            def mix_in(m):
                f = MIX_IN[m]
                act.wait_ge(nt_ready, FT + m + 1)
                if m >= 4:
                    act.wait_ge((n_lo_p, n_lo)[m % 2], HF + m // 2 - 1)
                act.activation((hp_p, hp_d)[m % 2][m // 2 % 2][:, PAD:PAD + NT], t_buf[m % 2][:, :], ACT.Identity,
                               bias=mod[1][:, f:f + 1]).then_inc(hp_ready, 1)

            act.wait_ge(dn_out, 16 * NI)
            for m in range(4):
                mix_in(m)
            for m in range(FT):
                act.wait_ge((pooled_p, pooled)[m % 2], m // 2 + 1)
                act.activation(h_hi[:, MIX_IN[m], :], (hp_p, hp_d)[m % 2][m // 2 % 2][:, PAD:PAD + NT], ACT.Copy).then_inc(n_hi, 1)
                if m % 2 and m + 4 <= FT:
                    mix_in(m + 3); mix_in(m + 4)
            for n_ in range(2 * FT):
                m = n_ // 2
                f = MIX_OUT[m]
                act.wait_ge(pl_ps, n_ + 1)
                if n_ >= 4:
                    act.wait_ge(pl_out, n_ - 3)
                act.activation(t_buf[m % 2][:, n_ % 2 * HALF:(n_ % 2 + 1) * HALF], ps[:, n_ % 4, :], ACT.Identity,
                               bias=gb[:, f:f + 1], scale=gs[:, f:f + 1]).then_inc(pl_t, 1)
                if n_ % 2 and m >= 1:
                    act.wait_ge(pl_out, 2 * m)
                    square(2, m - 1)
            act.wait_ge(pl_out, 2 * FT)
            square(2, FT - 1)
            norm_std(2)
            norm_hi(2, mod[1], 3 * FT)
            act.dma_start(fn_bc[:, :], final_norm.rearrange("(a n) -> a n", a=1).to_broadcast((P, D))).then_inc(fn_in, 16)
            act.wait_ge(n_lo, 3 * HF)
            act.wait_ge(n_lo_p, 3 * HF)
            ffn(1)
            for f in range(FT):
                act.wait_ge(dn_out, 16 * (2 * NI - 1) + 2 * f + 2)
                square(3, f)
            norm_std(3)

        @block.vector
        def _(dve):
            chain = [0]

            def link(ins):
                chain[0] += 1
                ins.then_inc(vstep, 1)
                dve.wait_ge(vstep, chain[0])

            dve.memset(one[:, :], 1.0).then_inc(cst_init, 1)
            dve.memset(eps[:, :], EPS).then_inc(cst_init, 1)
            dve.wait_ge(rows_t, 1)
            dve.tensor_copy(cst[:, :], ps[:, 6, 0:2 * MT + 7 * FT + NCONV]).then_inc(cst_ready, 1)

            def ada(u, c0=0):
                if u < EARLY:
                    dve.wait_ge(adae_in[u], 16)
                else:
                    dve.wait_ge(ada_in[u % 2], 16 * ((u - EARLY) // 2 + 1))
                if u == 1:
                    dve.wait_ge(csil_ready, 1)
                if u >= EARLY and acc_at(u)[1] is not None:
                    dve.wait_ge(ada_sum, acc_at(u)[1] + 1)
                dst = (acc_c if c0 else acc_x)[u // 2] if u < EARLY else acc_at(u)[0]
                src = ada_e[u] if u < EARLY else ada_raw[u % 2]
                for t in range(FT):
                    w, s_ = src[:, t, :], csil[:, c0 + t:c0 + t + 1]
                    if t == 0:
                        ins = dve.tensor_scalar(dst[:, :], w, s_, None, ALU.mult)
                    else:
                        ins = dve.scalar_tensor_tensor(out=dst[:, :], in0=w, scalar=s_, in1=dst[:, :],
                                                       op0=ALU.mult, op1=ALU.add)
                    if t < FT - 1:
                        link(ins)
                ins.then_inc(acc_dve, 1)

            def norm_gain(dst, w0, scale):
                return dve.scalar_tensor_tensor(out=dst[:, :], in0=scale, scalar=1.0,
                                                in1=cst[:, C_NW + w0 * FT:C_NW + (w0 + 1) * FT],
                                                op0=ALU.add, op1=ALU.mult)

            def rotary_tables():
                dve.wait_ge(gain_in, 32)
                dve.wait_ge(rope_in, 32)
                for n_ in range(2):
                    g = gains[:, n_:n_ + 1, :]
                    dve.tensor_tensor(tabs[2 * n_][:, :, :], cosT[:, :, :], g.to_broadcast((P, TT, HD)), ALU.mult)
                    for r in range(2):
                        for s_ in range(2):
                            o0, i0 = 32 * r + 16 * s_, 32 * r + 16 * (1 - s_)
                            ins = dve.tensor_tensor(tabs[2 * n_ + 1][:, :, o0:o0 + 16], sinT[:, :, o0:o0 + 16],
                                                    gains[:, n_:n_ + 1, i0:i0 + 16].to_broadcast((P, TT, 16)), ALU.mult)
                ins.then_inc(tab_ready, 1)

            for u in range(1, EARLY, 2):
                ada(u)
                if u == U_BOTH:
                    ada(u, FT)
                if u == 3:
                    dve.wait_ge(x_sq, TT + 1)
                    dve.reciprocal(rstd[:, 0:TT], std[:, 0:TT]).then_inc(x_rstd, 1)
                    rotary_tables()
            dve.wait_ge(ada_sum, EARLY)
            dve.wait_ge(cst_ready, 1)
            link(dve.tensor_tensor(mod[0][:, 0:2 * FT], ps[:, 7, 0:2 * FT], cst[:, 0:2 * FT], ALU.add))
            norm_gain(nA[0], 0, mod[0][:, FT:2 * FT]).then_inc(mod_ready, 1)

            for n_ in range(3 * FT):
                f, part = n_ % FT, n_ // FT
                w = HALF if part < 2 else NC
                hi = h_hi[:, f, part * HALF:part * HALF + w] if part < 2 else ch_hi[:, f, :]
                lo = h_lo[:, f, part * HALF:part * HALF + w] if part < 2 else ch_lo[:, f, :]
                if n_ == CTX_AT:
                    dve.wait_ge(x_sq, KT + 2)
                    dve.reciprocal(rstd[:, TT:KT], std[:, TT:KT]).then_inc(x_rstd, 1)
                if n_ == MODC_AT:
                    dve.wait_ge(adac_sum, 1)
                    link(dve.tensor_tensor(modc[:, :], ps[:, 7, MT:MT + 2 * FT], cst[:, 0:2 * FT], ALU.add))
                    norm_gain(nA[1], 0, modc[:, FT:2 * FT]).then_inc(mod_ready, 1)
                dve.wait_ge(t_ready, n_ + 1)
                if n_ == 0:
                    dve.wait_ge(acc_pool, NE - 2)
                if n_ == 2 * FT:
                    dve.wait_ge(xt_ready, 2 * FT)
                link(dve.tensor_copy(hi, t0[n_ % 2][:, 0:w]))
                dve.tensor_tensor(lo, t0[n_ % 2][:, 0:w], hi.bitcast(fp32), ALU.subtract).then_inc(h_split, 1)

            def k_lo(j):
                dve.wait_ge(k_hi_ready, 2 * j + 1)
                dve.tensor_tensor(ka[j % 2][HD:2 * HD, :], wide(5, 3)[0:HD, 0:NK],
                                  ka[j % 2][0:HD, :].bitcast(fp32), ALU.subtract).then_inc(k_lo_ready, 1)

            dve.wait_ge(tab_ready, 1)
            kq, vb = 0, 0
            for b, (u, p) in enumerate(BLKS):
                if b == MOD_AT:
                    dve.wait_ge(ada_sum, U_WA)
                    dve.tensor_tensor(mod[0][:, 2 * FT:2 * U_WA], ps[:, 7, 2 * FT:2 * U_WA], cst[:, 2 * FT:2 * U_WA], ALU.add
                                      ).then_inc(mod_ready, 1)
                if b == len(BLKS) - 1:
                    k_lo(0)
                if u == U_V:
                    if vb == 0:
                        dve.wait_ge(roped, kq)
                        dve.memset(v_hl[:, :, :, HD:HD + 2].bitcast(fp32), 1.0)
                    dve.wait_ge(v_hi_ready, vb + 1)
                    dve.tensor_tensor(v_hl[:, 2 * p:2 * p + 2, :, HD + 2:VW],
                                      heads(ps[:, b % 4, :].rearrange("p (a n) -> p a n", a=2)),
                                      v_hl[:, 2 * p:2 * p + 2, :, 0:HD].bitcast(fp32), ALU.subtract).then_inc(v_out, 1)
                    vb += 1
                else:
                    dst = k_tok[:, 2 * p:2 * p + 2, :] if u == U_K else q_tok[:, 2 * p:2 * p + 2, (u - U_Q) * UC:(u - U_Q + 1) * UC]
                    s1h = s1[:, :].rearrange("p (a d) -> p a d", d=HD)
                    dve.wait_ge(kq_out, kq + 1)
                    dve.tensor_reduce(ss[:, 0:8], s1h, AX.X, ALU.add).then_inc(ssq_ready, 1)
                    dve.wait_ge(kq_std, kq + 1)
                    link(dve.reciprocal(rstd[:, 0:8], std[:, 0:8]))
                    dh = heads(dst)
                    link(dve.tensor_tensor(dh, dh, rstd[:, 0:8].rearrange("p (a h o) -> p a h o", a=2, o=1)
                                           .to_broadcast((P, 2, 4, HD)), ALU.mult))
                    if u == U_K and p == NP_:
                        dve.tensor_tensor(dst.rearrange("p a (h d) -> p (a h) d", d=HD),
                                          dst.rearrange("p a (h d) -> p (a h) d", d=HD),
                                          gains[:, 1:2, :].to_broadcast((P, 8, HD)), ALU.mult).then_inc(roped, 1)
                    else:
                        cos, sin = (tabs[2], tabs[3]) if u == U_K else (tabs[0], tabs[1])
                        s1q = s1[:, :].rearrange("p (a h d) -> p a h d", a=2, d=HD)
                        dve.tensor_tensor(s1q, dh, cos[:, 2 * p:2 * p + 2, :].rearrange("p a (o d) -> p a o d", o=1)
                                          .to_broadcast((P, 2, 4, HD)), ALU.mult)
                        for a in range(2):
                            for s_ in range(2):
                                sv = s2[:, a * 256:(a + 1) * 256].rearrange("p (h r s i) -> p h r s i", h=4, r=2, s=2)
                                dv = dst[:, a, :].rearrange("p (h r s i) -> p h r s i", h=4, r=2, s=2)
                                tv = sin[:, 2 * p + a, :].rearrange("p (o r s i) -> p o r s i", o=1, r=2, s=2)
                                ins = dve.tensor_tensor(sv[:, :, :, s_, :], dv[:, :, :, 1 - s_, :],
                                                        tv[:, :, :, s_, :].to_broadcast((P, 4, 2, 16)), ALU.mult)
                        link(ins)
                        dve.tensor_tensor(dst, s1[:, :].rearrange("p (a n) -> p a n", a=2),
                                          s2[:, :].rearrange("p (a n) -> p a n", a=2), ALU.add).then_inc(roped, 1)
                    kq += 1
                if ADA_AT.get(b) in DVE_ADA:
                    ada(ADA_AT[b])

            dve.wait_ge(id_ready, 2)
            dve.tensor_copy(id_r[:, :], ident[:, :]).then_inc(id_ready, 1)

            def q_lo(h):
                dve.wait_ge(q_hi_ready, 2 * h + 1)
                dve.tensor_tensor(qb[h % 2][0:HD, :], wide(6)[0:HD, :],
                                  qa[h % 2][0:HD, :].bitcast(fp32), ALU.subtract).then_inc(q_lo_ready, 1)

            def maxes(h, n_):
                t, piece = divmod(n_, 3)
                w = min(HALF, NK - piece * HALF)
                g = (h - 1) * NM + n_
                dve.wait_ge(mx_ps, g + 1)
                dve.tensor_reduce(mx[h % 2][:, n_:n_ + 1], ps[:, 6 + g % 2, 0:w], AX.X, ALU.max).then_inc(mx_red, 1)

            def neg_max(h):
                if h > 0:
                    dve.wait_ge(mx_red, h * NM)
                    link(dve.tensor_reduce(mxr[:, :], mx[h % 2][:, :].rearrange("p (t k) -> p t k", k=3), AX.X, ALU.max))
                else:
                    dve.wait_ge(mx0_red, TT)
                dve.tensor_scalar(mneg[h % 2][:, :], mxr[:, :], -1.0, None, ALU.mult).then_inc(mneg_ready, 1)

            def p_low(s):
                dve.wait_ge(phi_ready, s + 1)
                dve.tensor_tensor(p_lo[s % 3][:, 0:LC], p32[s % 2][:, 0:LC], p_hi[s % 3][:, 0:LC].bitcast(fp32),
                                  ALU.subtract).then_inc(plo_ready, 1)

            def o_norm(n_):
                h, hf = divmod(n_, 2)
                dve.wait_ge(o_turned, n_ + 1)
                src = ps[:, 5, 0:4 * (HD + 2)].rearrange("p (t d) -> p t d", d=HD + 2)
                link(dve.reciprocal(rden[:, :].rearrange("p (t o) -> p t o", o=1), src[:, :, HD:HD + 1]))
                dve.tensor_tensor(q_tok[:, 4 * hf:4 * hf + 4, h * HD:(h + 1) * HD], src[:, :, 0:HD],
                                  rden[:, :].rearrange("p (t o) -> p t o", o=1).to_broadcast((P, 4, HD)),
                                  ALU.mult).then_inc(o_ready, 1)

            q_lo(0)
            for t in range(TT):
                dve.wait_ge(mx0_ps, t + 1)
                dve.tensor_reduce(mxr[:, t:t + 1], wide(3 * (t % 2), 3)[:, 0:NK], AX.X, ALU.max).then_inc(mx0_red, 1)
            neg_max(0)
            p_low(0)
            q_lo(1)
            for n_ in range(3):
                maxes(1, n_)
            for s in range(NH * NS):
                h, e = divmod(s, NS)
                if s > 0 and new_k(s - 1) is not None:
                    k_lo(new_k(s - 1))
                late_q = s > 0 and new_q(s - 1)[0] is not None and not new_q(s - 1)[1]
                if late_q:
                    q_lo(h + 2)
                g, ns = pieces(s)
                early = 0 if late_q else 1
                for n_ in ns[0:early]:
                    maxes(g, n_)
                if s + 1 < NH * NS:
                    p_low(s + 1)
                if new_q(s)[1]:
                    q_lo(h + 2)
                for n_ in ns[early:3]:
                    maxes(g, n_)
                if ns and ns[-1] == NM - 1:
                    neg_max(g)
                if s % HS == 1 and s > HS:
                    o_norm(s // HS - 1)
            o_norm(2 * NH - 1)

            for n_ in range(2 * FT):
                f, hf = n_ // 2, n_ % 2
                dve.wait_ge(oT_hi, n_ + 1)
                dve.tensor_tensor(h_lo[:, f, hf * HALF:(hf + 1) * HALF], ps[:, n_ % 4, :],
                                  h_hi[:, f, hf * HALF:(hf + 1) * HALF].bitcast(fp32), ALU.subtract).then_inc(oT_lo, 1)
            def add_square(k, m):
                R = len(SQ[k]) - 1
                dve.wait_ge(sq_ready, k * FT + m + 1)
                if m > 1:
                    dve.wait_ge(sq_added, k * (FT - 1) + m - 1)
                dve.tensor_tensor(SQ[k][0][:, :], SQ[k][0][:, :], SQ[k][(m - 1) % R + 1][:, :], ALU.add).then_inc(sq_added, 1)

            for g in range(NG):
                f, hf = g // 2, g % 2
                dve.wait_ge(wo_ps, g + 1)
                if g < 2 * FT:
                    dve.wait_ge(xr_out, FT + f + hf)
                xs = xT[:, f, hf * HALF:(hf + 1) * HALF]
                dve.scalar_tensor_tensor(out=xs, in0=ps[:, g % 4, :], scalar=mod[0][:, 2 * FT + f:2 * FT + f + 1],
                                         in1=xs, op0=ALU.mult, op1=ALU.add).then_inc(wo_out, 1)
                for u in WO_ADA.get(g, ()):
                    ada(u)
                if hf and f >= 2:
                    add_square(0, f - 1)
            add_square(0, FT - 1)
            dve.wait_ge(ada_sum, U_FA)
            dve.tensor_tensor(mod[1][:, 0:2 * NA1], ps[:, 7, 0:2 * NA1], cst[:, MT:MT + 2 * NA1], ALU.add).then_inc(adaf_out, 1)
            link(dve.tensor_tensor(mod[0][:, 2 * U_WA:MT], ps[:, 7, 2 * U_WA:MT], cst[:, 2 * U_WA:MT], ALU.add))
            norm_gain(nA[2], 1, mod[0][:, 4 * FT:5 * FT]).then_inc(mod_ready, 1)

            def norm_rstd(k):
                dve.wait_ge(ss_std, k + 1)
                dve.reciprocal(rstd[:, 0:TT], std[:, 0:TT]).then_inc(ss_rstd, 1)

            def norm_t(k, m, A_):
                f = MIX_IN[m] if k == 1 else m
                R = 2 if k == 1 else 4
                if m == 0:
                    dve.wait_ge(bc_ready, k + 1)
                if m >= R:
                    if k == 1:
                        dve.wait_ge(hp_ready, m - 1)
                    else:
                        dve.wait_ge((n_lo, n_lo_p)[m % 2], k * HF + (m - 4) // 2 + 1)
                dve.scalar_tensor_tensor(out=t_buf[m % R][:, :], in0=xT[:, f, :], scalar=A_[:, f:f + 1],
                                         in1=wide(6), op0=ALU.mult, op1=ALU.mult).then_inc(nt_ready, 1)

            def norm_split(k, A_, S_, c0):
                norm_rstd(k)
                norm_t(k, 0, A_)
                norm_t(k, 1, A_)
                for f in range(0, FT, 2):
                    if f + 2 < FT:
                        norm_t(k, f + 2, A_)
                    dve.wait_ge(n_hi, k * FT + f + 1)
                    dve.scalar_tensor_tensor(out=h_lo[:, f, :], in0=t_buf[f % 4][:, :], scalar=S_[:, c0 + f:c0 + f + 1],
                                             in1=h_hi[:, f, :].bitcast(fp32), op0=ALU.add, op1=ALU.subtract).then_inc(n_lo, 1)
                    if f + 3 < FT:
                        norm_t(k, f + 3, A_)

            def ffn(l):
                ub, hb, db = 4 * NI * l, 2 * NI * l, 16 * NI * l
                g2 = mod[l][:, 5 * FT:6 * FT]

                def conv(j, gate, i):
                    n_ = i * 4 + (ub + 2 * gate + j)
                    q = HT * gate + j
                    t = (y_gate if gate else y_val)[j]
                    up = wide(2 * j)
                    dve.wait_ge(y_ready, n_ + 1)
                    dve.scalar_tensor_tensor(out=t[:, 1:NT], in0=up[:, 0:NT - 1],
                                             scalar=cst[:, bass.ds(i * 2 + (CV_W[0] + q), 1)],
                                             in1=t[:, 1:NT], op0=ALU.mult, op1=ALU.add).then_inc(cv_half, 1)
                    dve.wait_ge(cv_half, n_ + 1)
                    dve.scalar_tensor_tensor(out=t[:, 0:NT - 1], in0=up[:, 1:NT],
                                             scalar=cst[:, bass.ds(i * 2 + (CV_W[2] + q), 1)],
                                             in1=t[:, 0:NT - 1], op0=ALU.mult, op1=ALU.add).then_inc(cv_done, 1)

                def down(i, n0=0, n1=2 * FT, last=False):
                    for n_ in range(n0, n1):
                        f, hf = n_ // 2, n_ % 2
                        xs = xT[:, f, hf * HALF:(hf + 1) * HALF]
                        dve.wait_ge(dn_ps, i * 16 + (db + n_ + 1))
                        dve.scalar_tensor_tensor(out=xs, in0=ps[:, 4 + n_ % 4, :], scalar=g2[:, f:f + 1],
                                                 in1=xs, op0=ALU.mult, op1=ALU.add).then_inc(dn_out, 1)
                        if last and hf and f >= 2:
                            add_square(2 * l + 1, f - 1)
                    if last:
                        add_square(2 * l + 1, FT - 1)

                def gated(i, hi=g_hi, lo=g_lo):
                    gate_product(i)
                    gate_lo(i, hi, lo)

                def gate_product(i):
                    for j in range(2):
                        dve.wait_ge(silu_ready, i * 2 + (hb + j + 1))
                        dve.tensor_tensor(y_gate[j][:, :], y_gate[j][:, :], y_val[j][:, :], ALU.mult).then_inc(g_ready, 1)

                def gate_lo(i, hi, lo):
                    for j in range(2):
                        dve.wait_ge(g_hi_ready, i * 2 + (hb + j + 1))
                        dve.tensor_tensor(lo[:, j, :], y_gate[j][:, :], hi[:, j, :].bitcast(fp32),
                                          ALU.subtract).then_inc(g_lo_ready, 1)

                def ada_out(i):
                    dve.wait_ge(adaf_sum, i)
                    dve.tensor_tensor(mod[1][:, bass.ds(i * 4 + (2 * NA1 - 4), 4)], ps[:, 4, 0:4],
                                      cst[:, bass.ds(i * 4 + (MT + 2 * NA1 - 4), 4)], ALU.add).then_inc(adaf_out, 1)

                conv(0, 0, 0); conv(1, 0, 0); conv(0, 1, 0); conv(1, 1, 0)
                gated(0)
                conv(0, 0, 1); conv(1, 0, 1)
                down(0)
                if l == 0:
                    ada_out(1)
                conv(0, 1, 1); conv(1, 1, 1)
                gated(1)
                with dve.Fori(2, NI - 1) as i:
                    conv(0, 0, i); conv(1, 0, i)
                    down(i - 1)
                    if l == 0:
                        ada_out(i)
                    conv(0, 1, i); conv(1, 1, i)
                    gated(i)
                i = NI - 1
                conv(0, 0, i); conv(1, 0, i); conv(0, 1, i); conv(1, 1, i)
                down(i - 1, 0, 6)
                gate_product(i)
                down(i - 1, 6, 10)
                gate_lo(i, g2_hi, g2_lo)
                down(i - 1, 10)
                if l == 0:
                    ada_out(i)
                down(i, last=True)

            dve.wait_ge(wo_out, NG)
            norm_split(0, nA[2], mod[0], 3 * FT)
            ffn(0)
            dve.wait_ge(adaf_out, NI)
            norm_gain(nA[3], 2, mod[1][:, FT:2 * FT])
            norm_gain(nA[4], 3, mod[1][:, 4 * FT:5 * FT])
            link(dve.tensor_tensor(gs[:, :], mod[1][:, 2 * FT:3 * FT], cst[:, C_PS:C_PS + FT], ALU.mult))
            link(dve.tensor_tensor(gb[:, :], gs[:, :], cst[:, C_PB:C_PB + FT], ALU.mult))
            dve.sem_inc(mod_ready, 1)
            norm_rstd(1)

            def t_(m):
                return lambda: norm_t(1, m, nA[3])

            def conv_constants():
                dve.wait_ge(rows_t, 2)
                dve.tensor_copy(cst[:, C_CV:C_CV + NCONV], ps[:, 5, 0:NCONV]).then_inc(cst_ready, 1)

            mix_tiles(dve, win_d, hp_d, HF, pmdstep, pooled, n_lo,
                      [[t_(0), t_(1), t_(2)], [t_(3), t_(4), t_(5)], [conv_constants], [t_(6), t_(7)]])
            for n_ in range(2 * FT):
                f, hf = MIX_OUT[n_ // 2], n_ % 2
                xs = xT[:, f, hf * HALF:(hf + 1) * HALF]
                dve.wait_ge(pl_t, n_ + 1)
                dve.tensor_tensor(xs, xs, t_buf[n_ // 2 % 2][:, hf * HALF:(hf + 1) * HALF], ALU.add).then_inc(pl_out, 1)
                if hf and n_ >= 5:
                    add_square(2, n_ // 2 - 1)
            add_square(2, FT - 1)
            norm_split(2, nA[4], mod[1], 3 * FT)
            ffn(1)
            norm_rstd(3)
            dve.wait_ge(fn_in, 16)
            for t in range(TT):
                dve.wait_ge(fin_ps, t + 1)
                if t == 0:
                    dve.wait_ge(ss_rstd, 4)
                if t >= 4:
                    dve.wait_ge(out_done[t % 4], 16 * (t // 4))
                dve.scalar_tensor_tensor(out=o_sb[t % 4][:, :], in0=wide(2 + 2 * (t % 3)), scalar=rstd[:, t:t + 1],
                                         in1=fn_bc[:, :], op0=ALU.mult, op1=ALU.mult).then_inc(fin_out, 1)

        @block.tensor
        def _(pe):
            def product(dst, terms, first=True, last=True):
                n_ = len(terms)
                for k, (ah, al, bh, bl) in enumerate(terms):
                    pe.matmul(dst, ah, bh, start=(k == 0 and first), stop=False)
                    pe.matmul(dst, ah, bl, start=False, stop=False)
                    mm = pe.matmul(dst, al, bh, start=False, stop=(k == n_ - 1 and last))
                return mm

            pe.wait_ge(rows_in, 16 * 8)
            pe.wait_ge(id_ready, 2)
            pe.transpose(ps[:, 6, 0:2 * MT], rows[0:2 * MT, 0, :], ident[0:2 * MT, 0:2 * MT])
            pe.transpose(ps[:, 6, 2 * MT:2 * MT + 7 * FT], rows[0:7 * FT, 1, :], ident[0:7 * FT, 0:7 * FT])
            pe.transpose(ps[:, 6, C_CV:C_CV + 4 * HT], rows[0:4 * HT, 2, :], ident[0:4 * HT, 0:4 * HT])
            pe.transpose(ps[:, 6, C_CV + 4 * HT:C_CV + 8 * HT], rows[0:4 * HT, 3, :], ident[0:4 * HT, 0:4 * HT]).then_inc(rows_t, 1)

            def ada(u):
                if u == 0:
                    pe.wait_ge(cst_init, 2)
                    pe.wait_ge(csil_ready, 1)
                if u == EARLY:
                    pe.wait_ge(mod_ready, 2)
                v = u % NU
                if u < EARLY and u % 2 == 0:
                    pe.wait_ge(adae_in[u], 16)
                    for j in range(UC // P):
                        q = 2 * v + j
                        for t in range(FT):
                            mm = pe.matmul(ps[:, 7, q:q + MT + 1:MT], ada_e[u][:, t, j * P:(j + 1) * P],
                                           csil[:, t:t + FT + 1:FT], start=t == 0, stop=t == FT - 1)
                    mm.then_inc(ada_sum, 1)
                    return
                if u < EARLY:
                    pe.wait_ge(acc_dve, u // 2 + 1 + (u > U_BOTH))
                else:
                    pe.wait_ge(*acc_of(u))
                src = acc_x[u // 2] if u < EARLY else acc_at(u)[0]
                for j in range(UC // P):
                    mm = pe.matmul(ps[:, 7, 2 * v + j:2 * v + j + 1], src[:, j * P:(j + 1) * P],
                                   one[:, :], start=True, stop=True)
                mm.then_inc(ada_sum, 1)

            for u in range(EARLY):
                ada(u)

            def turn_x(n_):
                f, part = n_ % FT, n_ // FT
                if n_ == 0:
                    pe.wait_ge(cst_ready, 1)
                if n_ % FT == 0:
                    pe.wait_ge(x_scaled, TT // 2 * (part + 1) if part < 2 else KT)
                if n_ >= 3:
                    pe.wait_ge(t_ready, n_ - 2)
                for t in range(TT // 2 if part < 2 else CT):
                    src = x_tok[:, part * TT // 2 + t, f * P:(f + 1) * P] if part < 2 else c_tok[:, t, f * P:(f + 1) * P]
                    mm = pe.transpose(ps[:, 4 + n_ % 3, t * P:(t + 1) * P], src, ident[:, :])
                mm.then_inc(xt_ready, 1)

            for n_ in range(FT + 3):
                turn_x(n_)
            for b, (u, p) in enumerate(BLKS):
                if u < U_WO and (b == 0 or BLKS[b - 1][0] != u):
                    pe.wait_ge(w_split, u + 1)
                if u == U_K:
                    pe.wait_ge(h_split, FT * (p // (NP_ // 2) + 1))
                if b >= 4:
                    c_ = b - 4
                    if BLKS[c_][0] == U_V:
                        pe.wait_ge(v_out, VB.index(c_) + 1)
                    else:
                        pe.wait_ge(kq_out, KQ.index(c_) + 1)
                bh, bl = hl(SLOT[u])
                for a in range(2):
                    t = 2 * p + a
                    if p < NP_:
                        terms = [(h_hi[:, k, t * P:(t + 1) * P], h_lo[:, k, t * P:(t + 1) * P], bh[:, k, :], bl[:, k, :]) for k in range(FT)]
                    else:
                        terms = [(ch_hi[:, k, a * P:(a + 1) * P], ch_lo[:, k, a * P:(a + 1) * P], bh[:, k, :], bl[:, k, :]) for k in range(FT)]
                    mm = product(ps[:, b % 4, a * UC:(a + 1) * UC], terms)
                mm.then_inc(blk, 1)
                if b == 0:
                    pe.wait_ge(acc_pool, NE - 1)
                    for v in range(1, EARLY, 2):
                        for j in range(UC // P):
                            mm = pe.matmul(ps[:, 7, MT + 2 * v + j:MT + 2 * v + j + 1], acc_c[v // 2][:, j * P:(j + 1) * P],
                                           one[:, :], start=True, stop=True)
                    mm.then_inc(adac_sum, 1)
                for n_ in TURN_AT.get(b, ()):
                    turn_x(n_)
                if b - 2 in ADA_AT:
                    ada(ADA_AT[b - 2])

            def turn_k(j):
                for t in range(KT):
                    mm = pe.transpose(wide(5, 3)[0:HD, t * P:(t + 1) * P], k_tok[:, t, j * HD:(j + 1) * HD], ident[:, :])
                mm.then_inc(kT_ready, 1)

            def turn_q(h):
                for t in range(TT):
                    mm = pe.transpose(wide(6)[0:HD, t * P:(t + 1) * P], q_tok[:, t, h * HD:(h + 1) * HD], ident[:, :])
                mm.then_inc(qT_ready, 1)

            def max_scores(h, n_):
                t, piece = divmod(n_, 3)
                w = min(HALF, NK - piece * HALF)
                g = (h - 1) * NM + n_
                if n_ == 0:
                    pe.wait_ge(q_hi_ready, 2 * h + 2)
                    pe.wait_ge(q_lo_ready, h + 1)
                    pe.wait_ge(k_lo_ready, h // GQ + 1)
                if g >= 2:
                    pe.wait_ge(mx_red, g - 1)
                pe.matmul(ps[:, 6 + g % 2, 0:w], qa[h % 2][:, t * P:(t + 1) * P],
                          ka[h // GQ % 2][:, piece * HALF:piece * HALF + w], start=True, stop=True).then_inc(mx_ps, 1)

            def max_row(h):
                pe.wait_ge(mneg_ready, h + 1)
                for t in range(TT):
                    mm = pe.matmul(wide(6)[0:1, t * P:(t + 1) * P], mneg[h % 2][:, t:t + 1], id_r[:, :], start=True, stop=True)
                mm.then_inc(mrow_ps, 1)

            def scores(s, a):
                h, e = divmod(s, NS)
                hf, kp = divmod(e, HS)
                if a == 0:
                    if e == 0:
                        pe.wait_ge(mrow_ready, h + 1)
                        if h % GQ == 0:
                            pe.wait_ge(k_hi_ready, 2 * (h // GQ) + 2)
                    if s >= 2:
                        pe.wait_ge(p_ready, s - 1)
                A_, B_ = ka[h // GQ % 2], kb[h // GQ % 2]
                qs = slice(hf * HALF, (hf + 1) * HALF)
                ks = slice((2 * kp + a) * P, (2 * kp + a + 1) * P)
                dst = ps[:, 2 * (s % 2) + a, :]
                pe.matmul(dst, A_[:, ks], qa[h % 2][:, qs], start=True, stop=False)
                pe.matmul(dst, B_[0:HD + 1, ks], qb[h % 2][0:HD + 1, qs], start=False, stop=True).then_inc(s_ps, 1)

            def values(s, a):
                h, e = divmod(s, NS)
                hf, kp = divmod(e, HS)
                j = h // GQ
                if a == 0:
                    if kp == 0 and s > 0:
                        pe.wait_ge(o_copied, s // HS)
                    pe.wait_ge(plo_ready, s + 1)
                    pe.wait_ge(plo2_ready, s + 1)
                t = 2 * kp + a
                v1, v2 = v_hl[:, t, j, 0:HD + 1], v_hl[:, t, j, HD + 2:VW]
                cs = slice(a * HALF, (a + 1) * HALF)
                st = kp == 0 and a == 0
                en = kp == HS - 1 and a == 1
                pe.matmul(ps[0:HD + 1, 4, :], v1, p_hi[s % 3][:, cs], start=st, stop=False, skip_group_check=True)
                pe.matmul(ps[0:HD, 4, :], v2, p_hi[s % 3][:, cs], start=False, stop=False, skip_group_check=True)
                mm = pe.matmul(ps[0:HD + 1, 4, :], v1, p_lo[s % 3][:, cs], start=False, stop=en, skip_group_check=True)
                if a == 1:
                    mm.then_inc(pv_step, 1)

            def turn_o(n_):
                pe.wait_ge(o_copied, n_ + 1)
                if n_ >= 1:
                    pe.wait_ge(o_ready, n_)
                for t in range(4):
                    mm = pe.transpose(ps[:, 5, t * (HD + 2):t * (HD + 2) + HD + 1], o_t[n_ % 2][0:HD + 1, t * P:(t + 1) * P],
                                      ident[0:HD + 1, 0:HD + 1])
                mm.then_inc(o_turned, 1)

            pe.wait_ge(roped, 2 * NP_ + 1)
            pe.wait_ge(mod_ready, 3)
            turn_k(0)
            pe.wait_ge(k_lo_ready, 1)
            turn_q(0)
            pe.wait_ge(q_hi_ready, 2)
            pe.wait_ge(q_lo_ready, 1)
            pe.wait_ge(v_out, len(VB))
            pe.wait_ge(kq_out, len(KQ))
            for t in range(TT):
                if t >= 2:
                    pe.wait_ge(mx0_red, t - 1)
                for piece in range(3):
                    w = min(HALF, NK - piece * HALF)
                    mm = pe.matmul(ps[:, 3 * (t % 2) + piece, 0:w], qa[0][:, t * P:(t + 1) * P],
                                   ka[0][:, piece * HALF:piece * HALF + w], start=True, stop=True)
                mm.then_inc(mx0_ps, 1)
            pe.wait_ge(id_ready, 3)
            max_row(0)
            pe.wait_ge(mx0_red, TT)
            pe.wait_ge(ones_ready, 2)
            for s in range(2):
                scores(s, 0); scores(s, 1)
            pe.wait_ge(mrow_ready, 1)
            turn_q(1)
            for n_ in range(3):
                max_scores(1, n_)
            for s in range(NH * NS):
                h, e = divmod(s, NS)
                g, ns = pieces(s)
                q, mid = new_q(s)
                cut = (0, 0) if s > 0 and new_q(s - 1)[0] is not None and not new_q(s - 1)[1] else (1, 2)
                if mid:
                    pe.wait_ge(mrow_ready, h + 2)
                    turn_q(q)
                if s + 2 < NH * NS:
                    scores(s + 2, 0)
                    for n_ in ns[0:cut[0]]:
                        max_scores(g, n_)
                    scores(s + 2, 1)
                if e == ROW and h + 1 < NH:
                    max_row(h + 1)
                values(s, 0)
                for n_ in ns[cut[0]:cut[1]]:
                    max_scores(g, n_)
                values(s, 1)
                for n_ in ns[cut[1]:3]:
                    max_scores(g, n_)
                if s % HS == 1 and s > HS:
                    turn_o(s // HS - 1)
                if new_k(s) is not None:
                    pe.wait_ge(mrow_ready, h + 2)
                    pe.wait_ge(o_ready, 2 * h + 1)
                    turn_k(new_k(s))
                if q is not None and not mid:
                    pe.wait_ge(k_lo_ready, q // GQ + 1)
                    turn_q(q)
            turn_o(2 * NH - 1)

            def norm_sum(k):
                pe.wait_ge(sq_added, (k + 1) * (FT - 1))
                for t in range(TT):
                    mm = pe.matmul(ps[:, S_BANK[k], t:t + 1], SQ[k][0][:, t * P:(t + 1) * P], one[:, :],
                                   start=True, stop=True)
                mm.then_inc(sq_used, 1)

            for n_ in range(2 * FT):
                f, hf = n_ // 2, n_ % 2
                if n_ == 0:
                    pe.wait_ge(o_ready, 2 * NH)
                if n_ < 4:
                    pe.wait_ge(p_ready, NH * NS)
                else:
                    pe.wait_ge(oT_lo, n_ - 3)
                for t in range(4):
                    mm = pe.transpose(ps[:, n_ % 4, t * P:(t + 1) * P], q_tok[:, 4 * hf + t, f * P:(f + 1) * P], ident[:, :])
                mm.then_inc(oT_ps, 1)
            def turn_xre(n_):
                f, hf = n_ % FT, n_ // FT
                if f == 0:
                    pe.wait_ge(xre_in[hf], 16)
                if n_ >= 2:
                    pe.wait_ge(xr_out, n_ - 1)
                for t in range(4):
                    mm = pe.transpose(ps[:, 4 + n_ % 2, t * P:(t + 1) * P], x_re[hf][:, t, f * P:(f + 1) * P], ident[:, :])
                mm.then_inc(xr_ps, 1)

            for n_ in range(FT):
                turn_xre(n_)
            for g in range(NG):
                u, o, hf = U_WO + g // 4, g // 2 % 2, g % 2
                if g < FT:
                    turn_xre(FT + g)
                if g % 4 == 0:
                    pe.wait_ge(w_split, u + 1)
                if g < 4:
                    pe.wait_ge(oT_lo, 2 * FT)
                else:
                    pe.wait_ge(wo_out, g - 3)
                ah, al = hl(SLOT[u])
                cs, hs_ = slice(o * P, (o + 1) * P), slice(hf * HALF, (hf + 1) * HALF)
                product(ps[:, g % 4, :], [(ah[:, k, cs], al[:, k, cs], h_hi[:, k, hs_], h_lo[:, k, hs_]) for k in range(FT)]
                        ).then_inc(wo_ps, 1)
                if 0 <= g - 4 < NWA:
                    ada(U_WA + g - 4)
            norm_sum(0)

            def norm_spread(k):
                pe.wait_ge(ss_rstd, k + 1)
                for t in range(TT):
                    mm = pe.matmul(wide(6)[:, t * P:(t + 1) * P], rstd[:, t:t + 1].to_broadcast((P, P)), ident[:, :],
                                   start=True, stop=True)
                mm.then_inc(bc_ready, 1)

            def ffn(l):
                b, ub, hb, db = FB[l], 4 * NI * l, 2 * NI * l, 16 * NI * l

                def up(gate, i, u):
                    s = gate
                    ah, al = hl(s)
                    pe.wait_ge(w_split, u + 1)
                    for j in range(2):
                        n_ = i * 4 + (ub + 2 * gate + j)
                        if not (is_step(i, 0) and gate == 0 and l == 0):
                            pe.wait_ge(cv_done, n_ - 1)
                        cs = slice(j * P, (j + 1) * P)
                        for hf in range(2):
                            hs_ = slice(hf * HALF, (hf + 1) * HALF)
                            mm = product(ps[:, 2 * j + hf, :], [(ah[:, k, cs], al[:, k, cs], h_hi[:, k, hs_], h_lo[:, k, hs_]) for k in range(FT)])
                        mm.then_inc(up_ps, 1)

                def ada_sums(i):
                    pe.wait_ge(acc_pool, i * 2 + NPA)
                    pe.wait_ge(dn_out, i * 16 - 3)
                    for z in range(2):
                        for j in range(UC // P):
                            mm = pe.matmul(ps[:, 4, 2 * z + j:2 * z + j + 1], acc_f[z][:, j * P:(j + 1) * P],
                                           one[:, :], start=True, stop=True)
                    mm.then_inc(adaf_sum, 1)

                def down(i, u, slot=2, hi=g_hi, lo=g_lo, last=False):
                    ah, al = hl_down(slot)
                    if l == 0 and not is_step(i, 0):
                        pe.wait_ge(adaf_out, i + 1)
                    pe.wait_ge(w_split, u + 1)
                    pe.wait_ge(g_lo_ready, i * 2 + (hb + 2))
                    for n_ in range(16):
                        f, hf = n_ // 2, n_ % 2
                        if not (is_step(i, 0) and l == 0 and n_ < 4):
                            pe.wait_ge(dn_out, i * 16 + (db + n_ - 3))
                        fs, hs_ = slice(f * P, (f + 1) * P), slice(hf * HALF, (hf + 1) * HALF)
                        product(ps[:, 4 + n_ % 4, :], [(ah[:, k, fs], al[:, k, fs], hi[:, k, hs_], lo[:, k, hs_]) for k in range(2)]
                                ).then_inc(dn_ps, 1)
                    if last:
                        norm_sum(2 * l + 1)

                ah, al = hl(0)
                pe.wait_ge(w_split, b + 1)
                for k in range(FT):
                    pe.wait_ge((n_lo, n_lo_p)[k % 2], 2 * l * HF + k // 2 + 1)
                    for n_ in range(4):
                        cs, hs_ = slice(n_ // 2 * P, (n_ // 2 + 1) * P), slice(n_ % 2 * HALF, (n_ % 2 + 1) * HALF)
                        mm = product(ps[:, n_, :], [(ah[:, k, cs], al[:, k, cs], h_hi[:, k, hs_], h_lo[:, k, hs_])],
                                     first=k == 0, last=k == FT - 1)
                        if k == FT - 1 and n_ % 2:
                            mm.then_inc(up_ps, 1)
                up(1, 0, b + 1)
                up(0, 1, b + 2)
                down(0, b + 3)
                if l == 0:
                    ada_sums(1)
                up(1, 1, b + 4)
                with pe.Fori(2, NI - 1) as i:
                    up(0, i, i * 3 + (b - 1))
                    down(i - 1, i * 3 + b)
                    if l == 0:
                        ada_sums(i)
                    up(1, i, i * 3 + (b + 1))
                i = NI - 1
                up(0, i, i * 3 + (b - 1))
                up(1, i, i * 3 + (b + 1))
                down(i - 1, i * 3 + b)
                if l == 0:
                    ada_sums(i)
                down(i, b + 3 * NI - 1, 0, g2_hi, g2_lo, last=True)

            norm_spread(0)
            ffn(0)
            pe.wait_ge(dn_out, 16 * NI)
            pe.wait_ge(adaf_out, NI)
            norm_spread(1)
            pe.wait_ge(conv1_in, 48)
            pe.transpose(ps[:, 5, 0:4 * HT], rows1[0:4 * HT, 0, :], ident[0:4 * HT, 0:4 * HT])
            pe.transpose(ps[:, 5, 4 * HT:8 * HT], rows1[0:4 * HT, 1, :], ident[0:4 * HT, 0:4 * HT]).then_inc(rows_t, 1)
            pe.wait_ge(w_split, U_POOL + 1)
            ah, al = hl(SLOT[U_POOL])
            for n_ in range(2 * FT):
                m, hf = n_ // 2, n_ % 2
                f = MIX_OUT[m]
                g, o = f // 2, f % 2
                pe.wait_ge(n_lo_p if f < HF else n_lo, HF + f % HF // 2 * 2 + 2)
                if n_ >= 4:
                    pe.wait_ge(pl_t, n_ - 3)
                cs, hs_ = slice(o * P, (o + 1) * P), slice(hf * HALF, (hf + 1) * HALF)
                product(ps[:, n_ % 4, :], [(ah[:, 2 * g + k, cs], al[:, 2 * g + k, cs], h_hi[:, 2 * g + k, hs_], h_lo[:, 2 * g + k, hs_]) for k in range(2)]
                        ).then_inc(pl_ps, 1)
            norm_sum(2)
            norm_spread(2)
            ffn(1)
            pe.wait_ge(dn_out, 32 * NI)
            for t in range(TT):
                if t >= 3:
                    pe.wait_ge(fin_out, t - 2)
                for f in range(FT):
                    mm = pe.transpose(wide(2 + 2 * (t % 3))[:, f * P:(f + 1) * P], xT[:, f, t * P:(t + 1) * P], ident[:, :])
                mm.then_inc(fin_ps, 1)


_INS = ["x", "c", "ctx", "c_ctx", "ada_w", "ada_b", "norm_w", "attn_wqkv", "attn_q_gain", "attn_k_gain", "attn_wo",
        "pool_w", "pool_b", "pool_scale", "ffn_w_up", "ffn_conv_w", "ffn_conv_b", "ffn_w_down", "final_norm"]


def _tables(n_tokens, head_dim, grid_w=64, theta=10000.0, windows=(2, 4, 8, 16)):
    import numpy as np
    nf = head_dim // 4
    freqs = (np.float32(theta) ** (-np.arange(nf, dtype=np.float32) / np.float32(nf))).astype(np.float32)
    pos = np.arange(n_tokens)
    ang = [(v.astype(np.float32)[:, None] * freqs).astype(np.float32) for v in (pos // grid_w, pos % grid_w)]
    cos = np.concatenate([np.cos(a) for a in (ang[0], ang[0], ang[1], ang[1])], axis=1).astype(np.float32)
    sin = np.concatenate([-np.sin(ang[0]), np.sin(ang[0]), -np.sin(ang[1]), np.sin(ang[1])], axis=1).astype(np.float32)
    pad = windows[-1] // 2
    edge = np.ones((len(windows), 2, pad), np.float32)
    for g, w in enumerate(windows):
        for t in range(w // 2):
            edge[g, 0, t] = w / (t + w // 2)
            u = n_tokens - w // 2 + t
            edge[g, 1, t] = w / (min(u + w // 2 - 1, n_tokens - 1) - (u - w // 2) + 1)
    return cos, sin, edge.reshape(-1)


def kernel(**inputs):
    import numpy as _np
    import concourse.bacc as _bacc
    from concourse import mybir as _mybir
    from concourse.bass_utils import run_bass_kernel_spmd as _run

    nc = _bacc.Bacc("TRN2", target_bir_lowering=False, num_devices=1)
    arrays, args = {}, []
    cos, sin, edge = _tables(inputs["x"].shape[1], inputs["attn_q_gain"].shape[1])
    given = [(n, inputs[n]) for n in _INS] + [("rope_cos", cos), ("rope_sin", sin), ("pool_edge", edge)]
    for name, a in given:
        a = _np.ascontiguousarray(a)
        arrays[f"in_{name}_dram"] = a
        args.append(nc.dram_tensor(f"in_{name}_dram", a.shape, _mybir.dt.from_np(a.dtype), kind="ExternalInput").ap())
    args.append(nc.dram_tensor("out_0_dram", inputs["x"].shape, _mybir.dt.float32, kind="ExternalOutput").ap())
    hybrid_trunk(nc, *args)
    r = _run(nc, [arrays], core_ids=[0])
    return r.results[0]["out_0_dram"]
```
